# Optimizing a Trainium2 kernel written in Bass

```python
import math
import jax, jax.numpy as jnp
from jax import lax
import numpy as np

D_MODEL = 1024
BATCH = 1
SEQ = 128
DEPTH = 2
DEC_BATCH = 1
DEC_SEQ = 256
PAST_LEN = 128

GRID_W = 64
HEAD_DIM = 64
ATTN_HEADS = 8
ATTN_KV_HEADS = 2
ATTN_GROUP = ATTN_HEADS // ATTN_KV_HEADS
DIFF_HEADS = 4
DIFF_QK_DIM = 2 * HEAD_DIM
DIFF_V_DIM = 2 * HEAD_DIM
RWKV_HEADS = 8
RWKV_HEAD_DIM = 64
BRANCH_WIDTH = 512
W_LORA = 64
A_LORA = 64
G_LORA = 128
D_FF = 2816
Q_BLOCK = 128
N_BRANCH = 3
N_MOD = 9
ROPE_THETA = 10000.0
ROPE_AXIS_DIM = HEAD_DIM // 2
DEEPNORM_ALPHA = (2.0 * DEPTH) ** 0.25
DEEPNORM_BETA = (8.0 * DEPTH) ** -0.25
LN_EPS = 1e-5
RMS_EPS = 1e-6
RWKV_GN_EPS = 64e-5
A_Q_W = ATTN_HEADS * HEAD_DIM
A_KV_W = ATTN_KV_HEADS * HEAD_DIM
B_QK_W = DIFF_HEADS * DIFF_QK_DIM
B_V_W = DIFF_HEADS * DIFF_V_DIM
C_IN_W = 3 * BRANCH_WIDTH + 2 * W_LORA + 2 * A_LORA + G_LORA
IN_SPLITS = (N_BRANCH * D_MODEL, A_Q_W, A_KV_W, A_KV_W, B_QK_W, B_QK_W, B_V_W, C_IN_W)
IN_WIDTH = sum(IN_SPLITS)
C_SPLITS = (BRANCH_WIDTH, BRANCH_WIDTH, BRANCH_WIDTH, 2 * W_LORA, 2 * A_LORA, G_LORA)

kernel_name = 'hybrid_flow_prefix_trunk'

def _split(x, sizes):
    return jnp.split(x, np.cumsum(sizes)[:-1].tolist(), axis=-1)

def layer_norm(x, g, b):
    xf = x.astype(jnp.float32)
    mu = jnp.mean(xf, -1, keepdims=True)
    var = jnp.mean(jnp.square(xf - mu), -1, keepdims=True)
    return ((xf - mu) * lax.rsqrt(var + LN_EPS) * g + b).astype(x.dtype)

def rms_norm(x, g):
    xf = x.astype(jnp.float32)
    return (xf * lax.rsqrt(jnp.mean(xf * xf, -1, keepdims=True) + RMS_EPS) * g).astype(x.dtype)

def axial_rope(T):
    n_rows = T // GRID_W
    row = jnp.repeat(jnp.arange(n_rows), GRID_W).astype(jnp.float32)
    col = jnp.tile(jnp.arange(GRID_W), n_rows).astype(jnp.float32)
    inv = 1.0 / (ROPE_THETA ** (jnp.arange(0, ROPE_AXIS_DIM, 2, dtype=jnp.float32) / ROPE_AXIS_DIM))
    ang = jnp.stack([row[:, None] * inv, col[:, None] * inv], axis=1)
    return jnp.cos(ang), jnp.sin(ang)

def apply_rope(x, cos, sin):
    shp = x.shape
    xr = x.astype(jnp.float32).reshape(shp[:-1] + (2, 2, ROPE_AXIS_DIM // 2))
    x1, x2 = xr[..., 0, :], xr[..., 1, :]
    out = jnp.stack([x1 * cos - x2 * sin, x2 * cos + x1 * sin], axis=-2)
    return out.reshape(shp).astype(x.dtype)

def map_query_blocks(fn, *qs):
    Tq = qs[0].shape[-2]
    nb = Tq // Q_BLOCK
    blocks = tuple(jnp.moveaxis(q.reshape(q.shape[:-2] + (nb, Q_BLOCK, q.shape[-1])), -3, 0) for q in qs)
    out = lax.map(lambda b: fn(*b), blocks)
    out = jnp.moveaxis(out, 0, -3)
    return out.reshape(out.shape[:-3] + (Tq, out.shape[-1]))

def _gqa_block(q, k, v):
    s = jnp.einsum('bhgqd,bhkd->bhgqk', q, k).astype(jnp.float32) * HEAD_DIM ** -0.5
    p = jax.nn.softmax(s, axis=-1).astype(v.dtype)
    return jnp.einsum('bhgqk,bhkd->bhgqd', p, v)

def _diff_block(q1, q2, k1, k2, v, lam):
    sc = HEAD_DIM ** -0.5
    s1 = jnp.einsum('bhqd,bhkd->bhqk', q1, k1).astype(jnp.float32) * sc
    s2 = jnp.einsum('bhqd,bhkd->bhqk', q2, k2).astype(jnp.float32) * sc
    p = jax.nn.softmax(s1, axis=-1) - lam * jax.nn.softmax(s2, axis=-1)
    return jnp.einsum('bhqk,bhkd->bhqd', p.astype(v.dtype), v)

def swiglu(x, w_in, w_out):
    a, b = jnp.split(x @ w_in, 2, axis=-1)
    return (jax.nn.silu(a) * b) @ w_out

def _rwkv_scan(S0, r, w, kk, a, k, v, reverse):
    def step(S, inp):
        r_t, w_t, kk_t, a_t, k_t, v_t = inp
        sa = jnp.einsum('bhvk,bhk->bhv', S, -kk_t)
        S = S * w_t[:, :, None, :] + sa[..., None] * (kk_t * a_t)[:, :, None, :] + v_t[..., None] * k_t[:, :, None, :]
        return S, jnp.einsum('bhvk,bhk->bhv', S, r_t)
    xs = tuple(jnp.moveaxis(t, 1, 0) for t in (r, w, kk, a, k, v))
    S, out = lax.scan(step, S0, xs, reverse=reverse)
    return S, jnp.moveaxis(out, 0, 1)

def rwkv7_bidir(cin, p, state0):
    B, T, _ = cin.shape
    f32 = jnp.float32
    prev = jnp.pad(cin[:, :-1], ((0, 0), (1, 0), (0, 0)))
    nxt = jnp.pad(cin[:, 1:], ((0, 0), (0, 1), (0, 0)))
    cin = cin + p['rwkv_mu'] * (0.5 * (prev + nxt) - cin)
    r, k, v, wl, al, gl = _split(cin, C_SPLITS)
    wl = wl.reshape(B, T, 2, W_LORA)
    al = al.reshape(B, T, 2, A_LORA)
    w_logit = (p['rwkv_w0'] + jnp.einsum('btdr,drc->btdc', jnp.tanh(wl), p['rwkv_w2'])).astype(f32)
    decay = jnp.exp(-jnp.exp(-jax.nn.softplus(-w_logit) - 0.5))
    a = jax.nn.sigmoid((p['rwkv_a0'] + jnp.einsum('btdr,drc->btdc', al, p['rwkv_a2'])).astype(f32))
    g = jax.nn.sigmoid(gl) @ p['rwkv_g2']
    heads = lambda t: t.reshape(t.shape[:-1] + (RWKV_HEADS, RWKV_HEAD_DIM))
    kk = heads(k * p['rwkv_k_k']).astype(f32)
    kk = kk * lax.rsqrt(jnp.sum(kk * kk, -1, keepdims=True) + 1e-12)
    k_h = heads(k[:, :, None, :] * (1.0 + (a - 1.0) * p['rwkv_k_a'])).astype(f32)
    a_h, w_h = heads(a), heads(decay)
    rh, vh = heads(r).astype(f32), heads(v).astype(f32)
    outs, states = [], []
    for d in range(2):
        S, o = _rwkv_scan(state0[:, d].astype(f32), rh, w_h[:, :, d], kk, a_h[:, :, d], k_h[:, :, d], vh, reverse=(d == 1))
        outs.append(o)
        states.append(S)
    o = outs[0] + outs[1]
    mu = jnp.mean(o, -1, keepdims=True)
    var = jnp.mean(jnp.square(o - mu), -1, keepdims=True)
    o = ((o - mu) * lax.rsqrt(var + RWKV_GN_EPS)).reshape(B, T, BRANCH_WIDTH) * p['rwkv_gn_g'] + p['rwkv_gn_b']
    bonus = jnp.sum(rh[:, :, None] * k_h * p['rwkv_r_k'], -1, keepdims=True) * vh[:, :, None]
    o = o + jnp.sum(bonus, axis=2).reshape(B, T, BRANCH_WIDTH)
    return (o * g).astype(cin.dtype), jnp.stack(states, axis=1)

def mixing_sublayer(h, p, lam_init, ctx):
    B, T, _ = h.shape
    gates, aq, ak, av, bq, bk, bv, cin = _split(h @ p['w_in'], IN_SPLITS)
    latent = ctx is not None
    if latent:
        cos, sin = axial_rope(T)
        rope = lambda t: apply_rope(t, cos, sin)
    else:
        rope = lambda t: t
    qa = rms_norm(aq.reshape(B, T, ATTN_KV_HEADS, ATTN_GROUP, HEAD_DIM), p['qk_norm_g'][0]).transpose(0, 2, 3, 1, 4)
    ka = rms_norm(ak.reshape(B, T, ATTN_KV_HEADS, HEAD_DIM), p['qk_norm_g'][1]).transpose(0, 2, 1, 3)
    va = av.reshape(B, T, ATTN_KV_HEADS, HEAD_DIM).transpose(0, 2, 1, 3)
    qb = bq.reshape(B, T, DIFF_HEADS, DIFF_QK_DIM).transpose(0, 2, 1, 3)
    kb = bk.reshape(B, T, DIFF_HEADS, DIFF_QK_DIM).transpose(0, 2, 1, 3)
    vb = bv.reshape(B, T, DIFF_HEADS, DIFF_V_DIM).transpose(0, 2, 1, 3)
    q1, q2 = rope(qb[..., :HEAD_DIM]), rope(qb[..., HEAD_DIM:])
    if latent:
        ctx_ka, ctx_va, ctx_kb, ctx_vb, state0 = ctx
        keys_a = jnp.concatenate([rope(ka), ctx_ka], axis=2)
        vals_a = jnp.concatenate([va, ctx_va], axis=2)
        k1 = jnp.concatenate([rope(kb[..., :HEAD_DIM]), ctx_kb[..., :HEAD_DIM]], axis=2)
        k2 = jnp.concatenate([rope(kb[..., HEAD_DIM:]), ctx_kb[..., HEAD_DIM:]], axis=2)
        vals_b = jnp.concatenate([vb, ctx_vb], axis=2)
    else:
        keys_a, vals_a = ka, va
        k1, k2 = kb[..., :HEAD_DIM], kb[..., HEAD_DIM:]
        vals_b = vb
        state0 = jnp.zeros((B, 2, RWKV_HEADS, RWKV_HEAD_DIM, RWKV_HEAD_DIM), jnp.float32)
    out_a = map_query_blocks(lambda q: _gqa_block(q, keys_a, vals_a), rope(qa))
    out_a = out_a.transpose(0, 3, 1, 2, 4).reshape(B, T, A_Q_W)
    lv = p['diff_lambda'].astype(jnp.float32)
    lam = jnp.exp(jnp.dot(lv[0], lv[1])) - jnp.exp(jnp.dot(lv[2], lv[3])) + lam_init
    out_b = map_query_blocks(lambda x1, x2: _diff_block(x1, x2, k1, k2, vals_b, lam), q1, q2)
    out_b = rms_norm(out_b, p['diff_subln_g']) * (1.0 - lam_init)
    out_b = out_b.transpose(0, 2, 1, 3).reshape(B, T, B_V_W)
    out_c, state = rwkv7_bidir(cin, p, state0)
    branches = jnp.stack([out_a, out_b, out_c], axis=2)
    up = jnp.einsum('btim,imd->btid', branches, p['w_up'])
    gate = jax.nn.sigmoid(gates.reshape(B, T, N_BRANCH, D_MODEL))
    out = jnp.sum(gate * up, axis=2) @ p['w_out']
    return out, (ka, va, kb, vb, state.astype(h.dtype))

def modulation(cvec, p):
    m = jax.nn.silu(cvec) @ p['w_mod'] + p['b_mod']
    return m.reshape(cvec.shape[0], N_MOD, D_MODEL)

def trunk_layer(x, mod, p, lam_init, ctx):
    m = lambda i: mod[:, None, i]
    adaln = lambda t, s: t * (1.0 + m(3 * s + 1)) + m(3 * s)
    h = swiglu(adaln(x, 0), p['ffn_w_in'][0], p['ffn_w_out'][0])
    x = layer_norm(DEEPNORM_ALPHA * x + 0.5 * m(2) * h, p['ln_g'][0], p['ln_b'][0])
    h, ctx_out = mixing_sublayer(adaln(x, 1), p, lam_init, ctx)
    x = layer_norm(DEEPNORM_ALPHA * x + m(5) * h, p['ln_g'][1], p['ln_b'][1])
    h = swiglu(adaln(x, 2), p['ffn_w_in'][1], p['ffn_w_out'][1])
    x = layer_norm(DEEPNORM_ALPHA * x + 0.5 * m(8) * h, p['ln_g'][2], p['ln_b'][2])
    return x, ctx_out

def setup_inputs(seed: int = 0) -> dict:
    key = jax.random.key(seed)
    ks = iter(jax.random.split(key, 40))
    nrm = lambda shape, s: jax.random.normal(next(ks), shape, jnp.float32) * s
    L, D = DEPTH, D_MODEL
    return {
        'x_prompt': nrm((BATCH, SEQ, D), 1.0),
        'x_sample': nrm((DEC_BATCH, DEC_SEQ, D), 1.0),
        'cache_attn_k': nrm((DEC_BATCH, L, ATTN_KV_HEADS, PAST_LEN, HEAD_DIM), 1.0),
        'cache_attn_v': nrm((DEC_BATCH, L, ATTN_KV_HEADS, PAST_LEN, HEAD_DIM), 1.0),
        'cache_diff_k': nrm((DEC_BATCH, L, DIFF_HEADS, PAST_LEN, DIFF_QK_DIM), 1.0),
        'cache_diff_v': nrm((DEC_BATCH, L, DIFF_HEADS, PAST_LEN, DIFF_V_DIM), 1.0),
        'state_rwkv': nrm((DEC_BATCH, L, 2, RWKV_HEADS, RWKV_HEAD_DIM, RWKV_HEAD_DIM), 0.3),
        'c': nrm((DEC_BATCH, D), 1.0),
        'c_ctx': nrm((D,), 1.0),
        'w_mod': nrm((L, D, N_MOD * D), 0.5 * D ** -0.5),
        'b_mod': nrm((L, N_MOD * D), 0.02),
        'ln_g': 1.0 + nrm((L, 3, D), 0.02),
        'ln_b': nrm((L, 3, D), 0.02),
        'ffn_w_in': nrm((L, 2, D, 2 * D_FF), D ** -0.5),
        'ffn_w_out': nrm((L, 2, D_FF, D), DEEPNORM_BETA * D_FF ** -0.5),
        'w_in': nrm((L, D, IN_WIDTH), D ** -0.5),
        'qk_norm_g': 1.0 + nrm((L, 2, HEAD_DIM), 0.02),
        'diff_lambda': nrm((L, 4, HEAD_DIM), 0.1),
        'diff_subln_g': 1.0 + nrm((L, DIFF_V_DIM), 0.02),
        'rwkv_mu': jax.random.uniform(next(ks), (L, C_IN_W), jnp.float32),
        'rwkv_w0': -2.0 + nrm((L, 2, BRANCH_WIDTH), 0.5),
        'rwkv_w2': nrm((L, 2, W_LORA, BRANCH_WIDTH), 0.1),
        'rwkv_a0': nrm((L, 2, BRANCH_WIDTH), 0.1),
        'rwkv_a2': nrm((L, 2, A_LORA, BRANCH_WIDTH), A_LORA ** -0.5),
        'rwkv_g2': nrm((L, G_LORA, BRANCH_WIDTH), G_LORA ** -0.5),
        'rwkv_k_k': 1.0 + nrm((L, BRANCH_WIDTH), 0.1),
        'rwkv_k_a': 1.0 + nrm((L, BRANCH_WIDTH), 0.1),
        'rwkv_r_k': nrm((L, RWKV_HEADS, RWKV_HEAD_DIM), 0.1),
        'rwkv_gn_g': 1.0 + nrm((L, BRANCH_WIDTH), 0.02),
        'rwkv_gn_b': nrm((L, BRANCH_WIDTH), 0.02),
        'w_up': nrm((L, N_BRANCH, BRANCH_WIDTH, D), BRANCH_WIDTH ** -0.5),
        'w_out': nrm((L, D, D), DEEPNORM_BETA * D ** -0.5),
    }

def reference(x_prompt, x_sample, cache_attn_k, cache_attn_v, cache_diff_k, cache_diff_v, state_rwkv, c, c_ctx,
              w_mod, b_mod, ln_g, ln_b, ffn_w_in, ffn_w_out, w_in, qk_norm_g, diff_lambda, diff_subln_g,
              rwkv_mu, rwkv_w0, rwkv_w2, rwkv_a0, rwkv_a2, rwkv_g2, rwkv_k_k, rwkv_k_a, rwkv_r_k,
              rwkv_gn_g, rwkv_gn_b, w_up, w_out):
    y_prompt, y_sample = x_prompt, x_sample
    n_ak, n_av, n_dk, n_dv, n_st = [], [], [], [], []
    for l in range(DEPTH):
        p = {'w_mod': w_mod[l], 'b_mod': b_mod[l], 'ln_g': ln_g[l], 'ln_b': ln_b[l],
             'ffn_w_in': ffn_w_in[l], 'ffn_w_out': ffn_w_out[l], 'w_in': w_in[l], 'qk_norm_g': qk_norm_g[l],
             'diff_lambda': diff_lambda[l], 'diff_subln_g': diff_subln_g[l], 'rwkv_mu': rwkv_mu[l],
             'rwkv_w0': rwkv_w0[l], 'rwkv_w2': rwkv_w2[l], 'rwkv_a0': rwkv_a0[l], 'rwkv_a2': rwkv_a2[l],
             'rwkv_g2': rwkv_g2[l], 'rwkv_k_k': rwkv_k_k[l], 'rwkv_k_a': rwkv_k_a[l], 'rwkv_r_k': rwkv_r_k[l],
             'rwkv_gn_g': rwkv_gn_g[l], 'rwkv_gn_b': rwkv_gn_b[l], 'w_up': w_up[l], 'w_out': w_out[l]}
        lam_init = 0.8 - 0.6 * math.exp(-0.3 * l)
        y_prompt, (ka, va, kb, vb, st) = trunk_layer(y_prompt, modulation(c_ctx[None], p), p, lam_init, None)
        n_ak.append(ka); n_av.append(va); n_dk.append(kb); n_dv.append(vb); n_st.append(st)
        ctx = (cache_attn_k[:, l], cache_attn_v[:, l], cache_diff_k[:, l], cache_diff_v[:, l], state_rwkv[:, l])
        y_sample, _ = trunk_layer(y_sample, modulation(c, p), p, lam_init, ctx)
    new_attn_k = jnp.stack(n_ak, axis=1)
    new_attn_v = jnp.stack(n_av, axis=1)
    new_diff_k = jnp.stack(n_dk, axis=1)
    new_diff_v = jnp.stack(n_dv, axis=1)
    new_state_rwkv = jnp.stack(n_st, axis=1)
    return (y_prompt, y_sample, new_attn_k, new_attn_v, new_diff_k, new_diff_v, new_state_rwkv)


_drawn_inputs = setup_inputs


def setup_inputs(seed=0):
    import zlib

    import numpy as np

    out = dict(_drawn_inputs(seed))
    spreads = {}
    factors = {'cache_attn_k': 8.0,
     'cache_attn_v': 8.0,
     'cache_diff_k': 3.491,
     'cache_diff_v': 3.125,
     'state_rwkv': 8.0,
     'qk_norm_g': 2.775,
     'diff_lambda': 8.0,
     'diff_subln_g': 37.1,
     'rwkv_r_k': 3.571,
     'rwkv_gn_g': 51.074,
     'rwkv_gn_b': 58.488}
    for name, (base, spread) in spreads.items():
        noise = np.random.default_rng([zlib.crc32(name.encode()), seed]).standard_normal(out[name].shape)
        drawn = base * np.exp(spread * noise) if base else spread * noise
        out[name] = __import__('jax').numpy.asarray(drawn.astype(out[name].dtype))
    for name, factor in factors.items():
        out[name] = (out[name] * factor).astype(out[name].dtype)
    return out
```

```python
import math
from contextlib import ExitStack

import numpy as np

import concourse.bass as bass
from concourse import mybir

ALU = mybir.AluOpType
ACT = mybir.ActivationFunctionType
AX_X = mybir.AxisListType.X
F32 = mybir.dt.float32
F32R = mybir.dt.float32r

D = 1024
KD = D // 128
DEPTH = 2
TP = 128
TS = 256
TOK = TP + TS
NCH = TOK // 128
PAST = 128
HD = 64
F = 2816
NF = F // 128
FH = 8
NBR = 3
N_MOD = 9
BW = 512
NB = BW // 128
GRID_W = 64
ALPHA = (2.0 * DEPTH) ** 0.25
LN_EPS = 1e-5
RMS_EPS = 1e-6
GN_EPS = 64e-5
KAPPA = math.exp(-0.5)
SCALE = HD ** -0.5
C_BLOCKS = 15
GROUPS = ((0, TP), (TP, TOK))
COL_AQ, COL_AK, COL_AV = 3072, 3584, 3712
COL_BQ, COL_BK, COL_BV, COL_C = 3840, 4352, 4864, 5376
LEVELS = (1, 2, 4, 8, 16, 32, 64)
ACC = 4
RAW, SPL, LOOK = 3, 4, 2
MODR = 3

CO_ID, CO_ONE, CO_BLK, CO_ROT, CO_SWAP = 0, 128, 256, 384, 512
CO_COS = 640
CO_SIN = CO_COS + TS
CO_LEV = CO_SIN + TS
CO_STR = CO_LEV + 2 * len(LEVELS) * 128
CO_INC = CO_STR + 256
CO_LAM = CO_INC + 256
CO_N = CO_LAM + 2 * DEPTH


def shape_constants():
    c = np.zeros((128, CO_N), np.float32)
    i = np.arange(128)
    c[:, CO_ID:CO_ID + 128] = np.eye(128)
    c[:, CO_ONE:CO_ONE + 128] = 1.0
    c[:, CO_BLK:CO_BLK + 128] = (i[:, None] // HD == i[None] // HD)
    for m in range(128):
        first = m % 32 < 16
        c[m + 16 if first else m - 16, CO_ROT + m] = -1.0 if first else 1.0
        c[(m + HD) % 128, CO_SWAP + m] = 1.0
    t = np.arange(TS)
    row, col = (t // GRID_W).astype(np.float32), (t % GRID_W).astype(np.float32)
    inv = (1.0 / (np.float32(10000.0) ** (np.arange(0, 32, 2, dtype=np.float32) / np.float32(32)))).astype(np.float32)
    for p in range(128):
        axis, f = (p % HD) // 32, p % 16
        ang = (row if axis == 0 else col) * inv[f]
        c[p, CO_COS:CO_COS + TS] = np.cos(ang)
        c[p, CO_SIN:CO_SIN + TS] = np.sin(ang)
    s, t = i[:, None], i[None]
    for d in range(2):
        a, b = (s, t) if d == 0 else (t, s)
        for n, size in enumerate(LEVELS):
            m = (a // (2 * size) == b // (2 * size)) & (a // size % 2 == 0) & (b // size % 2 == 1)
            o = CO_LEV + (d * len(LEVELS) + n) * 128
            c[:, o:o + 128] = m
        c[:, CO_STR + d * 128:CO_STR + d * 128 + 128] = a < b
        c[:, CO_INC + d * 128:CO_INC + d * 128 + 128] = a <= b
    for l in range(DEPTH):
        lam_init = 0.8 - 0.6 * math.exp(-0.3 * l)
        c[:, CO_LAM + 2 * l] = lam_init
        c[:, CO_LAM + 2 * l + 1] = 1.0 - lam_init
    return c


def plan_layer():
    chunks, groups, last = [], [], {}

    def ffn(f):
        for j in range(NF):
            for part in "ab":
                chunks.append((part, f, j))
                groups.append((part, f, j))
        for m in range(KD):
            chunks.extend(("o", f, m, c) for c in range(3))
            groups.append(("o", f, m))

    def one(*key):
        chunks.append(key)
        groups.append(key)

    ffn(0)
    for i in range(C_BLOCKS):
        one("c", i)
    for kind, n in (("aq", 4), ("ak", 1), ("bq", 4), ("bk", 4), ("av", 1), ("bv", 4)):
        for i in range(n):
            one(kind, i)
    for br in range(NBR):
        for mp in range(KD // 2):
            one("g", br, 2 * mp)
            one("g", br, 2 * mp + 1)
            chunks.append(("u", br, mp))
            groups.append(("u", br, 2 * mp))
            groups.append(("u", br, 2 * mp + 1))
    for m in range(KD):
        one("w", m)
    ffn(1)
    chunk_no = {k: n for n, k in enumerate(chunks)}
    for g in groups:
        last[g] = chunk_no[(g + (2,)) if g[0] == "o" else ("u", g[1], g[2] // 2) if g[0] == "u" else g]
    return chunk_no, {k: n for n, k in enumerate(groups)}, last


def plan_attention():
    units, n = [], 0
    for tile in range(2 * NB):
        mine = []
        for c in range(NCH):
            if tile < NB:
                for e in range(2):
                    mine.append({"c": c, "e": e, "sets": [(n, e)]})
                    n += 1
            else:
                mine.append({"c": c, "e": 0, "sets": [(n, 0), (n + 1, 1)]})
                n += 2
        for i, un in enumerate(mine):
            un.update(tile=tile, first=i == 0, last=i == len(mine) - 1, u=len(units))
            units.append(un)
    owner = {sn: un["u"] for un in units for sn, _ in un["sets"]}
    return units, owner


def mod_schedule():
    total = N_MOD * KD
    steps = 2 * NF
    first = 2 * KD
    return first, [min(total, first + -(-(total - first) * (i + 1) // steps)) for i in range(steps)]


def build(nc, I, O):
    chunk_no, group_no, group_end = plan_layer()
    units, set_unit = plan_attention()
    chunk_list = list(chunk_no)
    NCHUNK = len(chunk_list)
    mod_first, mod_after = mod_schedule()
    NMODC = N_MOD * KD
    qk_keys = [("aq", i) for i in range(4)] + [("ak", 0)] + [("bq", i) for i in range(4)] + [("bk", i) for i in range(4)]
    v_keys = [("av", 0)] + [("bv", i) for i in range(4)]

    def over(ap, n):
        return ap.rearrange("p (o w) -> p o w", o=1).to_broadcast([128, n, ap.shape[1]])

    glob = ExitStack()
    with glob:
        def sb(name, shape, dt=F32, ctx=glob):
            return ctx.enter_context(nc.sbuf_tensor(name, shape, dt))

        def sem(name):
            sems.append(glob.enter_context(nc.semaphore(name)))
            return sems[-1]

        sems = []

        cst = sb("cst", [128, CO_N])
        x = sb("x", [128, KD, TOK])
        xm_hi = sb("xm_hi", [128, KD, TOK], F32R)
        xm_lo = sb("xm_lo", [128, KD, TOK], F32R)
        raw = sb("raw", [128, RAW, 1024])
        w_hi = sb("w_hi", [128, SPL, 1024], F32R)
        w_lo = sb("w_lo", [128, SPL, 1024], F32R)
        par = sb("par", [128, 176])
        modv = sb("modv", [128, N_MOD, KD, 2])
        condT = sb("condT", [128, KD, 2])
        lam = sb("lam", [128, 8])
        small = sb("small", [128, 16])
        eps = sb("eps", [128, 4])
        ident = cst[:, CO_ID:CO_ID + 128]
        ones = cst[:, CO_ONE:CO_ONE + 128]
        blk = cst[:, CO_BLK:CO_BLK + 128]

        with ExitStack() as ph:
            h_hi = sb("h_hi", [128, NF, TOK], F32R, ph)
            h_lo = sb("h_lo", [128, NF, TOK], F32R, ph)
            modw = sb("modw", [128, MODR, 1024], ctx=ph)
            sa = sb("sa", [128, 2, TOK], ctx=ph)
            hf = sb("hf", [128, 2, TOK], ctx=ph)
            pst = sb("pst", [128, 2, 128], ctx=ph)
        with ExitStack() as ph:
            sq = sb("sq", [128, 4, TOK], ctx=ph)
            mean = sb("mean", [128, TOK], ctx=ph)
            rstd = sb("rstd", [128, TOK], ctx=ph)
            xrows = sb("xrows", [128, NCH, D], ctx=ph)
        with ExitStack() as mix:
            cmix = sb("cmix", [128, C_BLOCKS, TOK], ctx=mix)
            merged = sb("merged", [128, KD, TOK], ctx=mix)
            with ExitStack() as ph:
                br_hi = sb("br_hi", [128, NB, TOK], F32R, ph)
                br_lo = sb("br_lo", [128, NB, TOK], F32R, ph)
                sig = sb("sig", [128, 2, TOK], ctx=ph)
                gu = sb("gu", [128, 2, TOK], ctx=ph)
                cin = sb("cin", [128, 3, 388], ctx=ph)
                csum = sb("csum", [128, 2, 386], ctx=ph)
                qk = sb("qk", [128, 13, TOK], ctx=ph)
                kc = sb("kc", [128, 5, PAST], ctx=ph)
                kswap = sb("kswap", [128, TOK + PAST], ctx=ph)
                va = sb("va", [128, 4, 128], ctx=ph)
                vb = sb("vb", [128, 4, 512], ctx=ph)
                kst = sb("kst", [128, 5, 128], ctx=ph)
                pr = sb("pr", [128, 4, TOK], ctx=ph)
                pT = sb("pT", [128, 2, 3, 128], ctx=ph)
                t1 = sb("t1", [128, TOK], ctx=ph)
                t2 = sb("t2", [128, TOK], ctx=ph)
                t3 = sb("t3", [128, TOK], ctx=ph)
                st = sb("st", [128, 4, 4], ctx=ph)
            with ExitStack() as ph:
                brc_hi = sb("brc_hi", [128, NB, TOK], F32R, ph)
                brc_lo = sb("brc_lo", [128, NB, TOK], F32R, ph)
                sigc = sb("sigc", [128, 2, TOK], ctx=ph)
                guc = sb("guc", [128, 2, TOK], ctx=ph)
                lora_w = sb("lora_w", [128, BW], ctx=ph)
                lora_a = sb("lora_a", [128, BW], ctx=ph)
                lora_g = sb("lora_g", [128, BW], ctx=ph)
                vtok = sb("vtok", [128, NCH, BW], ctx=ph)
                kk = sb("kk", [128, TOK], ctx=ph)
                osum = sb("osum", [128, TOK], ctx=ph)
                ksum = sb("ksum", [128, TOK], ctx=ph)
                sg = sb("sg", [128, TOK], ctx=ph)
                aa = sb("aa", [128, TOK], ctx=ph)
                cs = sb("cs", [128, TOK], ctx=ph)
                zi = sb("zi", [128, TOK], ctx=ph)
                zx = sb("zx", [128, TOK], ctx=ph)
                half = sb("half", [128, NCH], ctx=ph)
                eh = sb("eh", [128, NCH], ctx=ph)
                ar = sb("ar", [128, NCH, 2, 128], ctx=ph)
                bt = sb("bt", [128, TOK], ctx=ph)
                kt = sb("kt", [128, TOK], ctx=ph)
                btok = sb("btok", [128, NCH, 128], ctx=ph)
                ktok = sb("ktok", [128, NCH, 128], ctx=ph)
                lt = sb("lt", [128, 6, 128], ctx=ph)
                ltm = sb("ltm", [128, 6, 128], ctx=ph)
                lak = sb("lak", [128, 6, 128], ctx=ph)
                rbk = sb("rbk", [128, 6, 2, 128], ctx=ph)
                xi = sb("xi", [128, 6, 128], ctx=ph)
                xt = sb("xt", [128, 6, 128], ctx=ph)
                tl = sb("tl", [128, 6, 64], ctx=ph)
                rs = sb("rs", [128, 128], ctx=ph)
                sas = sb("sas", [128, 128], ctx=ph)
                sld = sb("sld", [128, 128], ctx=ph)
                s0 = sb("s0", [128, 128], ctx=ph)
                sp = sb("sp", [128, 128], ctx=ph)
                spo = sb("spo", [128, 128], ctx=ph)
                spt = sb("spt", [128, 128], ctx=ph)

        acc = [glob.enter_context(nc.psum_tensor(f"acc{i}", [128, 512], F32)) for i in range(ACC)]
        pb = [glob.enter_context(nc.psum_tensor(f"pb{i}", [128, 512], F32)) for i in range(4)]

        raw_in = [sem(f"raw_in{i}") for i in range(RAW)]
        hi_done, lo_done, chunk_used = sem("hi_done"), sem("lo_done"), sem("chunk_used")
        acc_free = [sem(f"acc_free{i}") for i in range(ACC)]
        mod_in = [sem(f"mod_in{i}") for i in range(MODR)]
        mod_done, mod_read = sem("mod_done"), sem("mod_read")
        dch, ach, pch = sem("dve_chain"), sem("act_chain"), sem("pool_chain")
        par_in, par_t, par_done = sem("par_in"), sem("par_t"), sem("par_done")
        xf_ready, xhi_ready, xm_ready, scaled = sem("xf_ready"), sem("xhi_ready"), sem("xm_ready"), sem("scaled")
        silu_done, hhi_done, h_ready = sem("silu_done"), sem("hhi_done"), sem("h_ready")
        mean_done, d_ready, sq_ready, sq_used = sem("mean_done"), sem("d_ready"), sem("sq_ready"), sem("sq_used")
        std_done, n_ready, x_ready = sem("std_done"), sem("n_ready"), sem("x_ready")
        lam_in, lam_b, lam_dot, lam_exp, lam_done = (sem(n) for n in ("lam_in", "lam_b", "lam_dot", "lam_exp", "lam_done"))
        pads, cin_ready, csum_ready, cmix_ready = (sem(n) for n in ("pads", "cin_ready", "csum_ready", "cmix_ready"))
        qk_ready, qsq_ready, qms_done, qstd_done, qn_ready = (
            sem(n) for n in ("qk_ready", "qsq_ready", "qms_done", "qstd_done", "qn_ready"))
        rot_done, rope_ready, swap_done, swap_ready = (sem(n) for n in ("rot_done", "rope_ready", "swap_done", "swap_ready"))
        cache_in, kt_done, kc_ready = (sem(n) for n in ("cache_in", "kt_done", "kc_ready"))
        v_ready, kout_t, kout_ready, kv_out = (sem(n) for n in ("v_ready", "kout_t", "kout_ready", "kv_out"))
        scored, max_done, exp_done, probs_ready = (sem(n) for n in ("scored", "max_done", "exp_done", "probs_ready"))
        probs_t, probs_t_ready, weighted_done = (sem(n) for n in ("probs_t", "probs_t_ready", "weighted_done"))
        tile_read, branch_hi, branch_ready = (sem(n) for n in ("tile_read", "branch_hi", "branch_ready"))
        sub_sq, sub_ms, sub_std, sub_done = (sem(n) for n in ("sub_sq", "sub_ms", "sub_std", "sub_done"))
        sig_done, gated, merged_done, merged_hi = (sem(n) for n in ("sig_done", "gated", "merged_done", "merged_hi"))
        lora_in, lora_act, vtok_t, vtok_ready = (sem(n) for n in ("lora_in", "lora_act", "vtok_t", "vtok_ready"))
        kk_raw, kk_sq, kk_ms, kk_std, kk_ready = (sem(n) for n in ("kk_raw", "kk_sq", "kk_ms", "kk_std", "kk_ready"))
        lora_done, sg_done, z_ready, exps_done, ab_ready = (
            sem(n) for n in ("lora_done", "sg_done", "z_ready", "exps_done", "ab_ready"))
        tok_t, tok_ready, gram_done, gram_read = (sem(n) for n in ("tok_t", "tok_ready", "gram_done", "gram_read"))
        lt_ready = sem("lt_ready")
        ltm_ready, xt0_ready, xt_ready, xi_t, xi0_ready, xi_ready = (
            sem(n) for n in ("ltm_ready", "xt0_ready", "xt_ready", "xi_t", "xi0_ready", "xi_ready"))
        tl_done, tl_ready, u_done, xt_t = (sem(n) for n in ("tl_done", "tl_ready", "u_done", "xt_t"))
        state_in, state_t, sp_ready = (sem(n) for n in ("state_in", "state_t", "sp_ready"))
        r_done, r_ready, sa_done, sa_ready = (sem(n) for n in ("r_done", "r_ready", "sa_done", "sa_ready"))
        o_done, o_read, sn_done, sn_read = (sem(n) for n in ("o_done", "o_read", "sn_done", "sn_read"))
        spo_t, spo_ready, st_out = (sem(n) for n in ("spo_t", "spo_ready", "st_out"))
        gn_mean, gn_centred, gn_sq, gn_var, gn_std = (sem(n) for n in ("gn_mean", "gn_centred", "gn_sq", "gn_var", "gn_std"))
        bonus_in, bonus_sum, bonus_read, out_gate, out_done = (
            sem(n) for n in ("bonus_in", "bonus_sum", "bonus_read", "out_gate", "out_done"))
        brc_hi_s, brc_ready = sem("brc_hi_done"), sem("brc_ready")
        init_in, init_t, init_done, fin_t, fin_cp, y_out = (
            sem(n) for n in ("init_in", "init_t", "init_done", "fin_t", "fin_cp", "y_out"))

        def linker(eng, chain):
            count = {}

            def done(ins, s):
                count[s.name] = count.get(s.name, 0) + 1
                ins.then_inc(s, 1)
                eng.wait_ge(s, count[s.name])

            def link(ins):
                done(ins, chain)

            def freed(ins, key):
                ins.then_inc(free_sem(key), 1)
                wait_freed(eng, key)
            return link, done, freed

        def gbank(key):
            return acc[group_no[key] % ACC]

        def wait_group(eng, key):
            eng.wait_ge(chunk_used, group_end[key] + 1)

        def free_sem(key):
            return acc_free[group_no[key] % ACC]

        def wait_freed(eng, key):
            eng.wait_ge(free_sem(key), group_no[key] // ACC + 1)

        with nc.Block() as block:
            @block.sync
            def _(sy):
                sy.dma_start(cst[:, :], I["const"]).then_inc(init_in, 16)
                sy.dma_start(xrows[:, 0, :], I["x_prompt"][0]).then_inc(init_in, 16)
                sy.dma_start(xrows[:, 1:3, :], I["x_sample"][0].rearrange("(c p) d -> p c d", p=128)).then_inc(init_in, 16)
                sy.dma_start(sq[0:KD, 0, 0:128], I["c_ctx"].rearrange("(k p) -> k p", p=128)).then_inc(init_in, 16)
                sy.dma_start(sq[0:KD, 0, 128:256], I["c"][0].rearrange("(k p) -> k p", p=128)).then_inc(init_in, 16)

            @block.tensor
            def _(pe):
                pe.wait_ge(init_in, 80)
                for k in range(KD):
                    if k >= 4:
                        pe.wait_ge(init_done, k - 3)
                    for c in range(NCH):
                        mm = pe.transpose(pb[k % 4][:, c * 128:(c + 1) * 128], xrows[:, c, k * 128:(k + 1) * 128], ident)
                    mm.then_inc(init_t, 1)
                for g in range(2):
                    mm = pe.transpose(acc[0][:, g * KD:(g + 1) * KD], sq[0:KD, 0, g * 128:(g + 1) * 128], ident[0:KD, 0:KD])
                mm.then_inc(init_t, 1)

            @block.vector
            def _(dve):
                for i, e in enumerate((LN_EPS, RMS_EPS, GN_EPS, 1e-12)):
                    dve.memset(eps[:, i:i + 1], e)
                for k in range(KD):
                    dve.wait_ge(init_t, k + 1)
                    dve.tensor_copy(x[:, k, :], pb[k % 4][:, 0:TOK]).then_inc(init_done, 1)

            @block.scalar
            def _(act):
                act.wait_ge(init_t, KD + 1)
                act.activation(condT[:, :, :].rearrange("p k g -> p g k"),
                               acc[0][:, 0:2 * KD].rearrange("p (g k) -> p g k", g=2), ACT.Silu)

        with nc.Fori(0, DEPTH) as l:
            def lay(name):
                ap = I[name]
                return ap[bass.ds(l, 1)]

            def chunk_src(key):
                kind = key[0]
                if kind in "ab" and len(kind) == 1:
                    _, f, j = key
                    c0 = (0 if kind == "a" else F) + j * 128
                    return lay("ffn_w_in")[:, f, :, c0:c0 + 128].rearrange("l (k p) c -> p (l k) c", p=128), KD, 128
                if kind == "o":
                    _, f, m, c = key
                    nk = min(FH, NF - FH * c)
                    r0 = c * FH * 128
                    return (lay("ffn_w_out")[:, f, r0:r0 + nk * 128, m * 128:(m + 1) * 128]
                            .rearrange("l (k p) c -> p (l k) c", p=128), nk, 128)
                if kind == "u":
                    _, br, mp = key
                    return lay("w_up")[:, br, :, mp * 256:(mp + 1) * 256].rearrange("l (k p) c -> p (l k) c", p=128), NB, 256
                if kind == "w":
                    return lay("w_out")[:, :, key[1] * 128:(key[1] + 1) * 128].rearrange("l (k p) c -> p (l k) c", p=128), KD, 128
                base = {"c": COL_C, "aq": COL_AQ, "ak": COL_AK, "av": COL_AV, "bq": COL_BQ, "bk": COL_BK, "bv": COL_BV}
                c0 = key[1] * D + key[2] * 128 if kind == "g" else base[kind] + key[1] * 128
                return lay("w_in")[:, :, c0:c0 + 128].rearrange("l (k p) c -> p (l k) c", p=128), KD, 128

            def chunk_len(key):
                return (min(FH, NF - FH * key[3]) * 128) if key[0] == "o" else 1024

            with nc.Block() as block:
                @block.sync
                def _(sy):
                    v = lambda n: lay(n)
                    rows = [(pst[0:72, 0, :], v("b_mod").rearrange("l (k p) -> (l k) p", p=128)),
                            (pst[72:96, 0, :], v("ln_g").rearrange("l s (k p) -> (l s k) p", p=128)),
                            (pst[96:120, 0, :], v("ln_b").rearrange("l s (k p) -> (l s k) p", p=128)),
                            (pst[0:15, 1, :], v("rwkv_mu").rearrange("l (k p) -> (l k) p", p=128)),
                            (pst[15:23, 1, :], v("rwkv_w0").rearrange("l s (k p) -> (l s k) p", p=128)),
                            (pst[23:31, 1, :], v("rwkv_a0").rearrange("l s (k p) -> (l s k) p", p=128)),
                            (pst[31:35, 1, :], v("rwkv_k_k").rearrange("l (k p) -> (l k) p", p=128)),
                            (pst[35:39, 1, :], v("rwkv_k_a").rearrange("l (k p) -> (l k) p", p=128)),
                            (pst[39:43, 1, :], v("rwkv_r_k").rearrange("l (k h) d -> (l k) (h d)", h=2)),
                            (pst[43:47, 1, :], v("rwkv_gn_g").rearrange("l (k p) -> (l k) p", p=128)),
                            (pst[47:51, 1, :], v("rwkv_gn_b").rearrange("l (k p) -> (l k) p", p=128)),
                            (pst[51:52, 1, :], v("diff_subln_g")),
                            (pst[52:54, 1, 0:HD], v("qk_norm_g").rearrange("l s d -> (l s) d")),
                            (pst[52:54, 1, HD:128], v("qk_norm_g").rearrange("l s d -> (l s) d"))]

                    def load_mod(q):
                        if q >= MODR:
                            sy.wait_ge(mod_done, q - MODR + 1)
                        sy.dma_start(modw[:, q % MODR, :].rearrange("p (k c) -> p k c", k=KD),
                                     lay("w_mod")[:, :, q * 128:(q + 1) * 128].rearrange("l (k p) c -> p (l k) c", p=128)
                                     ).then_inc(mod_in[q % MODR], 16)

                    def load_chunk(key):
                        n = chunk_no[key]
                        src, nk, nc_ = chunk_src(key)
                        if n >= RAW:
                            sy.wait_ge(lo_done, n - RAW + 1)
                        sy.dma_start(raw[:, n % RAW, 0:nk * nc_].rearrange("p (k c) -> p k c", k=nk), src
                                     ).then_inc(raw_in[n % RAW], 16)

                    for q in range(MODR):
                        load_mod(q)
                    for dst, src in rows:
                        sy.dma_start(dst, src).then_inc(par_in, 16)
                    for q in range(MODR, mod_first):
                        load_mod(q)
                    done = mod_first
                    for i in range(2 * NF):
                        load_chunk(("ab"[i % 2], 0, i // 2))
                        for q in range(done, mod_after[i]):
                            load_mod(q)
                        done = mod_after[i]
                    mid = chunk_no[("c", 0)]
                    for n in range(2 * NF, mid + LOOK):
                        load_chunk(chunk_list[n])
                    sy.dma_start(small[:, 0:2], I["const"][:, bass.ds(l * 2 + CO_LAM, 2)]).then_inc(lam_in, 16)
                    sy.wait_ge(xm_ready, 2 * KD)
                    sy.dma_start(kst[:, 0, :].rearrange("p (h d) -> p h d", h=2),
                                 lay("cache_attn_k_l").rearrange("l h p d -> p (l h) d")).then_inc(cache_in, 16)
                    sy.dma_start(kst[:, 1:5, :], lay("cache_diff_k_l").rearrange("l h p d -> p (l h) d")).then_inc(cache_in, 16)
                    sy.dma_start(va[:, 3, :].rearrange("p (h d) -> p h d", h=2),
                                 lay("cache_attn_v_l").rearrange("l h p d -> p (l h) d")).then_inc(cache_in, 16)
                    sy.dma_start(vb[:, 3, :].rearrange("p (h d) -> p h d", h=4),
                                 lay("cache_diff_v_l").rearrange("l h p d -> p (l h) d")).then_inc(cache_in, 16)
                    sy.dma_start(pr[0:1, 0, 0:256], lay("diff_lambda").rearrange("l a d -> l (a d)")).then_inc(lam_in, 16)

                    vfirst = chunk_no[("g", 0, 0)]
                    for n in range(mid + LOOK, vfirst):
                        load_chunk(chunk_list[n])
                    for n in range(vfirst, vfirst + LOOK):
                        load_chunk(chunk_list[n])
                    for key in v_keys:
                        wait_freed(sy, key)
                    sy.dma_start(O["new_attn_v_l"][bass.ds(l, 1)].rearrange("l h p d -> p (l h) d"),
                                 va[:, 0, :].rearrange("p (h d) -> p h d", h=2)).then_inc(kv_out, 16)
                    sy.dma_start(O["new_diff_v_l"][bass.ds(l, 1)].rearrange("l h p d -> p (l h) d"),
                                 vb[:, 0, :].rearrange("p (h d) -> p h d", h=4)).then_inc(kv_out, 16)
                    sy.wait_ge(kout_ready, 2)
                    sy.dma_start(O["new_attn_k_l"][bass.ds(l, 1)].rearrange("l h p d -> p (l h) d"),
                                 kst[:, 0, :].rearrange("p (h d) -> p h d", h=2)).then_inc(kv_out, 16)
                    sy.dma_start(O["new_diff_k_l"][bass.ds(l, 1)].rearrange("l h p d -> p (l h) d"),
                                 kst[:, 1:5, :]).then_inc(kv_out, 16)
                    rwk = chunk_no[("g", 2, 0)]
                    for n in range(vfirst + LOOK, rwk + LOOK):
                        load_chunk(chunk_list[n])
                    sy.wait_ge(merged_done, 2 * KD)
                    sy.wait_ge(kv_out, 64)
                    sy.dma_start(lora_w[:, :], lay("rwkv_w2").rearrange("l s r c -> (l s r) c")).then_inc(lora_in, 16)
                    sy.dma_start(lora_a[:, :], lay("rwkv_a2").rearrange("l s r c -> (l s r) c")).then_inc(lora_in, 16)
                    sy.dma_start(lora_g[:, :], lay("rwkv_g2").rearrange("l r c -> (l r) c")).then_inc(lora_in, 16)
                    for n in range(rwk + LOOK, rwk + RAW):
                        load_chunk(chunk_list[n])
                    for g in range(2 * NB):
                        j, d = g // 2, g % 2
                        if g == 0:
                            sy.wait_ge(pads, 2)
                        else:
                            sy.wait_ge(state_t, g)
                        for hh in range(2):
                            sy.dma_start(sld[64 * hh:64 * hh + 64, 64 * hh:64 * hh + 64],
                                         lay("state_rwkv_l")[:, d, 2 * j + hh].rearrange("l v k -> (l v) k")
                                         ).then_inc(state_in, 16)
                        if g >= 1:
                            store_state = g - 1
                            jj, dd = store_state // 2, store_state % 2
                            sy.wait_ge(spo_ready, g)
                            for hh in range(2):
                                sy.dma_start(O["new_state_l"][bass.ds(l, 1), dd, 2 * jj + hh].rearrange("l v k -> (l v) k"),
                                             spt[64 * hh:64 * hh + 64, 64 * hh:64 * hh + 64]).then_inc(st_out, 16)
                    sy.wait_ge(spo_ready, 2 * NB)
                    for hh in range(2):
                        sy.dma_start(O["new_state_l"][bass.ds(l, 1), 1, 2 * (NB - 1) + hh].rearrange("l v k -> (l v) k"),
                                     spt[64 * hh:64 * hh + 64, 64 * hh:64 * hh + 64]).then_inc(st_out, 16)
                    for n in range(rwk + RAW, NCHUNK):
                        load_chunk(chunk_list[n])
                    sy.wait_ge(st_out, 16 * 4 * NB)

                @block.tensor
                def _(pe):
                    def open_group(key):
                        g = group_no[key]
                        if g >= ACC:
                            pe.wait_ge(acc_free[g % ACC], g // ACC)

                    def open_chunk(key):
                        pe.wait_ge(lo_done, chunk_no[key] + 1)

                    def weights(key, col):
                        s = chunk_no[key] % SPL
                        return w_hi[:, s, col:col + 128], w_lo[:, s, col:col + 128]

                    def mm3(out, lhs, rhs, first, last):
                        pe.matmul(out, lhs[0], rhs[0], start=first, stop=False)
                        pe.matmul(out, lhs[0], rhs[1], start=False, stop=False)
                        return pe.matmul(out, lhs[1], rhs[0], start=False, stop=last)

                    def xm_tile(k, t=slice(0, TOK)):
                        return xm_hi[:, k, t], xm_lo[:, k, t]

                    def project(key):
                        open_chunk(key)
                        open_group(key)
                        for k in range(KD):
                            mm = mm3(gbank(key)[:, 0:TOK], weights(key, k * 128), xm_tile(k), k == 0, k == KD - 1)
                        mm.then_inc(chunk_used, 1)

                    def project_by_token(key):
                        open_chunk(key)
                        open_group(key)
                        for c in range(NCH):
                            t = slice(c * 128, (c + 1) * 128)
                            for k in range(KD):
                                mm = mm3(gbank(key)[:, t], xm_tile(k, t), weights(key, k * 128), k == 0, k == KD - 1)
                        mm.then_inc(chunk_used, 1)

                    def mod_chunk(q):
                        pe.wait_ge(mod_in[q % MODR], 16 * (q // MODR + 1))
                        if q == mod_first:
                            pe.wait_ge(mod_read, 1)
                        for k in range(KD):
                            mm = pe.matmul(pb[0][:, 2 * q:2 * q + 2], modw[:, q % MODR, k * 128:(k + 1) * 128],
                                           condT[:, k, :], start=k == 0, stop=k == KD - 1)
                        mm.then_inc(mod_done, 1)

                    def layer_norm(s, keyf):
                        for m in range(KD):
                            wait_freed(pe, keyf(m))
                            mm = pe.matmul(pb[1][:, 0:TOK], ones, x[:, m, :], start=m == 0, stop=m == KD - 1)
                        mm.then_inc(mean_done, 1)
                        for m in range(KD):
                            pe.wait_ge(sq_ready, KD * s + m + 1)
                            pe.matmul(pb[2][:, 0:TOK], ones, sq[:, m % 4, :], start=m == 0, stop=m == KD - 1
                                      ).then_inc(sq_used, 1)

                    def ffn(f):
                        pe.wait_ge(xm_ready, KD * (1 if f == 0 else 4))
                        done = mod_first
                        for i in range(2 * NF):
                            project(("ab"[i % 2], f, i // 2))
                            if f == 0:
                                for q in range(done, mod_after[i]):
                                    mod_chunk(q)
                                done = mod_after[i]
                        for m in range(KD):
                            open_group(("o", f, m))
                            for c in range(3):
                                key = ("o", f, m, c)
                                open_chunk(key)
                                for k in range(c * FH, min(NF, (c + 1) * FH)):
                                    if m == 0:
                                        pe.wait_ge(h_ready, NF * f + k + 1)
                                    mm = mm3(gbank(key[:3])[:, 0:TOK], weights(key, (k - c * FH) * 128),
                                             (h_hi[:, k, :], h_lo[:, k, :]), k == 0, k == NF - 1)
                                mm.then_inc(chunk_used, 1)
                        layer_norm(2 * f, lambda m: ("o", f, m))

                    def branch(br, hi, lo):
                        for mp in range(KD // 2):
                            project(("g", br, 2 * mp))
                            project(("g", br, 2 * mp + 1))
                            key = ("u", br, mp)
                            open_chunk(key)
                            for e in range(2):
                                gk = ("u", br, 2 * mp + e)
                                open_group(gk)
                                for k in range(NB):
                                    mm = mm3(gbank(gk)[:, 0:TOK], weights(key, k * 256 + e * 128),
                                             (hi[:, k, :], lo[:, k, :]), k == 0, k == NB - 1)
                            mm.then_inc(chunk_used, 1)

                    pe.wait_ge(par_in, 16 * 14)
                    pe.transpose(pb[3][:, 0:120], pst[0:120, 0, :], ident[0:120, 0:120])
                    pe.transpose(pb[3][:, 120:174], pst[0:54, 1, :], ident[0:54, 0:54]).then_inc(par_t, 1)
                    for q in range(mod_first):
                        mod_chunk(q)
                    ffn(0)

                    pe.wait_ge(xm_ready, KD * 2)
                    for i in range(C_BLOCKS):
                        project(("c", i))
                    for kind, n in (("aq", 4), ("ak", 1), ("bq", 4), ("bk", 4)):
                        for i in range(n):
                            project((kind, i))
                    for kind, n in (("av", 1), ("bv", 4)):
                        for i in range(n):
                            project_by_token((kind, i))

                    pe.wait_ge(lam_in, 32)
                    pe.matmul(pb[3][:, 0:256], ones[0:1, :], pr[0:1, 0, 0:256], start=True, stop=True).then_inc(lam_b, 1)
                    pe.wait_ge(cache_in, 64)
                    for i in range(5):
                        if i == 4:
                            pe.wait_ge(kc_ready, 1)
                        mm = pe.transpose(pb[0][:, (i % 4) * 128:(i % 4 + 1) * 128], kst[:, i, :], ident)
                        if i >= 3:
                            mm.then_inc(kt_done, 1)
                    for i in range(5):
                        pe.wait_ge(qsq_ready, i + 1)
                        pe.matmul(pb[1][:, 0:TOK], blk, t1[:, :], start=True, stop=True).then_inc(qms_done, 1)
                    pe.wait_ge(lam_dot, 1)
                    for i in range(13):
                        if i < 5:
                            pe.wait_ge(qn_ready, i + 1)
                        else:
                            wait_freed(pe, qk_keys[i])
                        if i >= 2:
                            pe.wait_ge(rope_ready, i - 1)
                        pe.matmul(pb[2 + i % 2][:, 0:TS], cst[:, CO_ROT:CO_ROT + 128], qk[:, i, TP:TOK],
                                  start=True, stop=True).then_inc(rot_done, 1)
                    pe.wait_ge(rope_ready, 13)
                    pe.wait_ge(kc_ready, 2)
                    pe.matmul(pb[0][:, 0:TOK], cst[:, CO_SWAP:CO_SWAP + 128], qk[:, 4, :], start=True, stop=True)
                    pe.matmul(pb[0][:, TOK:TOK + PAST], cst[:, CO_SWAP:CO_SWAP + 128], kc[:, 0, :], start=True,
                              stop=True).then_inc(swap_done, 1)
                    for i in range(5):
                        if i == 4:
                            pe.wait_ge(kout_ready, 1)
                        mm = pe.transpose(pb[1][:, (i % 4) * 128:(i % 4 + 1) * 128], qk[:, (4, 9, 10, 11, 12)[i], 0:TP], ident)
                        if i >= 3:
                            mm.then_inc(kout_t, 1)
                    pe.wait_ge(swap_ready, 1)
                    pe.wait_ge(kout_ready, 2)
                    for key in v_keys:
                        wait_freed(pe, key)

                    def scores(un):
                        tile, c = un["tile"], un["c"]
                        for n, e in un["sets"]:
                            if n >= 2:
                                pe.wait_ge(exp_done, n - 1)
                            p = slice(HD * e, HD * e + HD)
                            if tile >= NB:
                                q, kn, kp = qk[p, 5 + tile - NB, :], qk[p, 9 + tile - NB, :], kc[p, 1 + tile - NB, :]
                            elif (2 * tile + e) // 4 == e:
                                q, kn, kp = qk[p, tile, :], qk[p, 4, :], kc[p, 0, :]
                            else:
                                q, kn, kp = qk[p, tile, :], kswap[p, 0:TOK], kswap[p, TOK:TOK + PAST]
                            q = q[:, c * 128:(c + 1) * 128]
                            if c == 0:
                                mm = pe.matmul(pb[n % 2][:, 0:TP], q, kn[:, 0:TP], start=True, stop=True)
                            else:
                                pe.matmul(pb[n % 2][:, 0:TS], q, kn[:, TP:TOK], start=True, stop=True)
                                mm = pe.matmul(pb[n % 2][:, TS:TOK], q, kp, start=True, stop=True)
                            mm.then_inc(scored, 1)

                    def weighted(un):
                        u, c, tile, e = un["u"], un["c"], un["tile"], un["e"]
                        nk = 1 if c == 0 else 3
                        slot = un["sets"][-1][0] % 4
                        pe.wait_ge(probs_ready, u + 1)
                        if u >= 1:
                            pe.wait_ge(probs_t_ready, u)
                        for k in range(nk):
                            mm = pe.transpose(pb[2][:, k * 128:(k + 1) * 128], pr[:, slot, k * 128:(k + 1) * 128], ident)
                        mm.then_inc(probs_t, 1)
                        pe.wait_ge(probs_t_ready, u + 1)
                        if un["first"] and tile > NB:
                            pe.wait_ge(sub_std, tile - NB)
                        elif un["first"] and tile >= 1:
                            pe.wait_ge(branch_ready, tile)
                        for k in range(nk):
                            tok = 0 if c == 0 else k + 1
                            if tile < NB:
                                kv = (2 * tile + e) // 4
                                vals = va[:, tok, HD * kv:HD * kv + HD]
                                out = pb[3][HD * e:HD * e + HD, c * 128:(c + 1) * 128]
                            else:
                                vals = vb[:, tok, (tile - NB) * 128:(tile - NB + 1) * 128]
                                out = pb[3][:, c * 128:(c + 1) * 128]
                            mm = pe.matmul(out, vals, pT[:, u % 2, k, :], start=k == 0, stop=k == nk - 1)
                        mm.then_inc(weighted_done, 1)
                        if un["last"] and tile >= NB:
                            pe.wait_ge(sub_sq, tile - NB + 1)
                            pe.matmul(pb[3][:, 0:TOK], ones, t1[:, :], start=True, stop=True).then_inc(sub_ms, 1)

                    def attention(mine):
                        prev = None
                        for un in mine:
                            scores(un)
                            if prev:
                                weighted(prev)
                            prev = un
                        weighted(prev)

                    attention([un for un in units if un["tile"] < NB])
                    pe.wait_ge(branch_ready, NB)
                    branch(0, br_hi, br_lo)
                    attention([un for un in units if un["tile"] >= NB])
                    pe.wait_ge(branch_ready, 2 * NB)
                    branch(1, br_hi, br_lo)

                    pe.wait_ge(cmix_ready, C_BLOCKS)
                    for c in range(NCH):
                        for j in range(NB):
                            mm = pe.transpose(pb[c][:, j * 128:(j + 1) * 128], cmix[:, 8 + j, c * 128:(c + 1) * 128], ident)
                        mm.then_inc(vtok_t, 1)
                    pe.wait_ge(vtok_ready, NCH)
                    pe.wait_ge(lora_in, 48)
                    pe.wait_ge(lora_act, 2)
                    for g in range(2 * NB):
                        j, d = g // 2, g % 2
                        ch = slice(j * 128, (j + 1) * 128)
                        dp = slice(64 * d, 64 * d + 64)
                        if d == 0:
                            pe.wait_ge(kk_sq, j + 1)
                            pe.matmul(pb[3][:, 0:TOK], blk, zi[:, :], start=True, stop=True).then_inc(kk_ms, 1)
                        pe.matmul(pb[0][:, 0:TOK], lora_w[dp, ch], cmix[dp, 12, :], start=True, stop=True)
                        pe.matmul(pb[1][:, 0:TOK], lora_a[dp, ch], cmix[dp, 13, :], start=True, stop=True
                                  ).then_inc(lora_done, 1)
                        pe.wait_ge(ab_ready, g + 1)
                        for c in range(NCH):
                            t = slice(c * 128, (c + 1) * 128)
                            pe.transpose(pb[0][:, t], bt[:, t], ident)
                            mm = pe.transpose(pb[1][:, t], kt[:, t], ident)
                        mm.then_inc(tok_t, 1)
                        if g >= 1:
                            pe.wait_ge(o_read, 3 * g)
                        for f in range(6):
                            n = 6 * g + f
                            if n >= 2:
                                pe.wait_ge(gram_read, n - 1)
                                pe.wait_ge(lt_ready, n - 1)
                            c, hh = f // 2, f % 2
                            hp = slice(64 * hh, 64 * hh + 64)
                            for i in range(2):
                                lhs = (bt, kt)[i][hp, c * 128:(c + 1) * 128]
                                mm = pe.matmul(pb[2 + n % 2][:, i * 256:(i + 1) * 256], lhs,
                                               ar[hp, c, :, :].rearrange("p a t -> p (a t)"), start=True, stop=True)
                            mm.then_inc(gram_done, 1)
                        pe.wait_ge(gram_read, 6 * g + 6)
                        pe.wait_ge(lt_ready, 6 * g + 6)
                        pe.wait_ge(tok_ready, g + 1)
                        pe.wait_ge(xt0_ready, g + 1)
                        for u in range(6):
                            mm = pe.transpose(pb[2 + u // 3][:, (u % 3) * 128:(u % 3 + 1) * 128], xt[:, u, :], ident)
                        mm.then_inc(xi_t, 1)
                        for n in range(1, len(LEVELS)):
                            lv = (len(LEVELS) - 1) * g + n
                            b = LEVELS[n]
                            pe.wait_ge(ltm_ready, len(LEVELS) * g + n + 1)
                            if n == 1:
                                pe.wait_ge(xi0_ready, g + 1)
                            else:
                                pe.wait_ge(xi_ready, lv - 1)
                            for u in range(6):
                                cols = xi[:, u, :].rearrange("p (q h b) -> p q h b", h=2, b=b)[:, :, d, :]
                                mm = pe.matmul(pb[0][:, u * 64:(u + 1) * 64], ltm[:, u, :], cols, start=True, stop=True)
                            mm.then_inc(tl_done, 1)
                            pe.wait_ge(tl_ready, lv)
                            if n > 1:
                                pe.wait_ge(xt_ready, lv - 1)
                            for u in range(6):
                                mm = pe.matmul(pb[1][:, u * 64:(u + 1) * 64], xt[:, u, :], tl[:, u, :], start=True, stop=True)
                            mm.then_inc(u_done, 1)
                            pe.wait_ge(xi_ready, lv)
                            for u in range(6):
                                mm = pe.transpose(pb[2 + u // 3][:, (u % 3) * 128:(u % 3 + 1) * 128], xi[:, u, :], ident)
                            mm.then_inc(xt_t, 1)
                        pe.wait_ge(xt_ready, (len(LEVELS) - 1) * (g + 1))
                        pe.wait_ge(state_in, 32 * (g + 1))
                        pe.transpose(pb[3][:, 0:128], sld[:, :], ident).then_inc(state_t, 1)
                        for i, c in enumerate((0, 1, 2) if d == 0 else (0, 2, 1)):
                            n = 3 * g + i
                            if i >= 1:
                                pe.wait_ge(sp_ready, 2 * g + i)
                            for hh in range(2):
                                if i >= 1:
                                    hs = slice(64 * hh, 64 * hh + 64)
                                    pe.matmul(pb[0][:, hs], ar[:, c, 0, :], sp[:, hs], start=True, stop=False)
                                v = vtok[:, c, j * 128 + 64 * hh:j * 128 + 64 * hh + 64]
                                mm = pe.matmul(pb[0][:, 64 * hh:64 * hh + 64], lak[:, 3 * hh + c, :], v,
                                               start=i == 0, stop=True)
                            mm.then_inc(r_done, 1)
                            pe.wait_ge(r_ready, n + 1)
                            for hh in range(2):
                                mm = pe.matmul(pb[1][:, 64 * hh:64 * hh + 64], xt[:, 3 * hh + c, :],
                                               rs[:, 64 * hh:64 * hh + 64], start=True, stop=True)
                            mm.then_inc(sa_done, 1)
                            pe.wait_ge(sa_ready, n + 1)
                            if n >= 1:
                                pe.wait_ge(o_read, n)
                            if i >= 1:
                                pe.matmul(pb[2][:, 0:128], sp[:, :], ar[:, c, 1, :], start=True, stop=False)
                            for hh in range(2):
                                hs = slice(64 * hh, 64 * hh + 64)
                                v = vtok[:, c, j * 128 + 64 * hh:j * 128 + 64 * hh + 64]
                                pe.matmul(pb[2][hs, 0:128], sas[:, hs], rbk[:, 3 * hh + c, 0, :], start=i == 0, stop=False)
                                mm = pe.matmul(pb[2][hs, 0:128], v, rbk[:, 3 * hh + c, 1, :], start=False, stop=True)
                            mm.then_inc(o_done, 1)
                            if i < 2:
                                pe.wait_ge(sp_ready, 2 * g + 1)
                                if i == 1:
                                    pe.wait_ge(spo_ready, g + 1)
                                for hh in range(2):
                                    hs = slice(64 * hh, 64 * hh + 64)
                                    v = vtok[:, c, j * 128 + 64 * hh:j * 128 + 64 * hh + 64]
                                    pe.matmul(pb[3][hs, hs], btok[:, c, hs], sas[:, hs], start=True, stop=False)
                                    mm = pe.matmul(pb[3][hs, hs], ktok[:, c, hs], v, start=False, stop=True)
                                mm.then_inc(sn_done, 1)
                                if i == 0:
                                    pe.wait_ge(sn_read, g + 1)
                                    pe.transpose(pb[3][:, 128:256], spo[:, :], ident).then_inc(spo_t, 1)
                        if d == 1:
                            pe.wait_ge(o_read, 3 * g + 3)
                            pe.matmul(pb[1][:, 0:TOK], blk, osum[:, :], start=True, stop=True).then_inc(gn_mean, 1)
                            pe.wait_ge(bonus_in, j + 1)
                            pe.matmul(pb[3][:, 0:TOK], blk, cs[:, :], start=True, stop=True).then_inc(bonus_sum, 1)
                            pe.matmul(pb[0][:, 0:TOK], lora_g[:, ch], cmix[:, 14, :], start=True, stop=True
                                      ).then_inc(out_gate, 1)
                            pe.wait_ge(gn_sq, j + 1)
                            pe.matmul(pb[2][:, 0:TOK], blk, zi[:, :], start=True, stop=True).then_inc(gn_var, 1)
                            pe.wait_ge(out_done, j + 1)
                    pe.wait_ge(brc_ready, NB)
                    branch(2, brc_hi, brc_lo)

                    pe.wait_ge(xm_ready, 2 * KD + KD)
                    for m in range(KD):
                        project(("w", m))
                    layer_norm(1, lambda m: ("w", m))
                    ffn(1)

                @block.scalar
                def _(act):
                    link, done, freed = linker(act, ach)
                    nsplit = [0]

                    def splits_to(n):
                        for c in range(nsplit[0], min(n + 1, NCHUNK)):
                            act.wait_ge(raw_in[c % RAW], 16 * (c // RAW + 1))
                            if c >= SPL:
                                act.wait_ge(chunk_used, c - SPL + 1)
                            w = chunk_len(chunk_list[c])
                            done(act.activation(w_hi[:, c % SPL, 0:w], raw[:, c % RAW, 0:w], ACT.Copy), hi_done)
                            nsplit[0] = c + 1

                    def ahead(key):
                        splits_to(chunk_no[key] + LOOK)

                    def xm_high(s, base):
                        for m in range(KD):
                            act.wait_ge(xf_ready, KD * s + m + 1)
                            done(act.activation(xm_hi[:, m, :], sq[:, m % 4, :], ACT.Copy), xhi_ready)

                    def h_high(f, j):
                        wait_freed(act, ("b", f, j))
                        done(act.activation(h_hi[:, j, :], hf[:, j % 2, :], ACT.Copy), hhi_done)

                    def ffn(f):
                        for j in range(NF):
                            ka, kb = ("a", f, j), ("b", f, j)
                            ahead(ka)
                            wait_group(act, ka)
                            if j >= 2:
                                wait_freed(act, ("b", f, j - 2))
                            freed(act.activation(sa[:, j % 2, :], gbank(ka)[:, 0:TOK], ACT.Silu), ka)
                            ahead(kb)
                            if j >= 1:
                                h_high(f, j - 1)
                        h_high(f, NF - 1)
                        for m in range(KD):
                            for c in range(3):
                                ahead(("o", f, m, c))

                    def layer_norm(s):
                        for m in range(KD):
                            act.wait_ge(d_ready, KD * s + m + 1)
                            if m >= 4:
                                act.wait_ge(sq_used, KD * s + m - 3)
                            done(act.activation(sq[:, m % 4, :], x[:, m, :], ACT.Square), sq_ready)
                        act.wait_ge(sq_used, KD * (s + 1))
                        done(act.activation(mean[:, :], pb[2][:, 0:TOK], ACT.Sqrt, scale=1.0 / D, bias=eps[:, 0:1]), std_done)
                        for m in range(KD):
                            act.wait_ge(n_ready, KD * s + m + 1)
                            done(act.activation(x[:, m, :], x[:, m, :], ACT.Identity, scale=par[:, 72 + KD * s + m:73 + KD * s + m],
                                           bias=par[:, 96 + KD * s + m:97 + KD * s + m]), x_ready)

                    def branch(br, sg_):
                        for mp in range(KD // 2):
                            for e in range(2):
                                m = 2 * mp + e
                                key = ("g", br, m)
                                ahead(key)
                                wait_group(act, key)
                                if br > 0 or m >= 2:
                                    wait_freed(act, ("u", br, m - 2) if m >= 2 else ("u", br - 1, m + KD - 2))
                                freed(act.activation(sg_[:, e, :], gbank(key)[:, 0:TOK], ACT.Sigmoid), key)
                            ahead(("u", br, mp))

                    splits_to(LOOK - 1)
                    xm_high(0, 0)
                    ffn(0)
                    layer_norm(0)
                    xm_high(1, 1)

                    act.wait_ge(pads, 1)
                    for i in range(C_BLOCKS):
                        key = ("c", i)
                        ahead(key)
                        wait_group(act, key)
                        if i >= 3:
                            act.wait_ge(cmix_ready, i - 2)
                        link(act.activation(cin[:, i % 3, 1:1 + TP], gbank(key)[:, 0:TP], ACT.Copy))
                        freed(act.activation(cin[:, i % 3, 3 + TP:3 + TOK], gbank(key)[:, TP:TOK], ACT.Copy), key)
                    for i, key in enumerate(qk_keys):
                        ahead(key)
                        wait_group(act, key)
                        freed(act.activation(qk[:, i, :], gbank(key)[:, 0:TOK], ACT.Copy), key)
                    for key in v_keys:
                        ahead(key)
                    act.wait_ge(lam_dot, 1)
                    done(act.activation(lam[:, 2:4], lam[:, 0:2], ACT.Exp), lam_exp)
                    for i in range(5):
                        wait_freed(act, qk_keys[i])
                        if i >= 1:
                            act.wait_ge(qms_done, i)
                        done(act.activation(t1[:, :], qk[:, i, :], ACT.Square), qsq_ready)
                        act.wait_ge(qms_done, i + 1)
                        if i >= 1:
                            act.wait_ge(qn_ready, i)
                        done(act.activation(t2[:, :], pb[1][:, 0:TOK], ACT.Sqrt, scale=1.0 / HD, bias=eps[:, 1:2]), qstd_done)

                    def finish(un):
                        u, tile = un["u"], un["tile"]
                        w = 128 if un["c"] == 0 else TOK
                        act.wait_ge(probs_t, u + 1)
                        if u >= 2:
                            act.wait_ge(weighted_done, u - 1)
                        done(act.activation(pT[:, u % 2, :, :].rearrange("p k t -> p (k t)")[:, 0:w], pb[2][:, 0:w], ACT.Copy
                                       ), probs_t_ready)
                        if not un["last"]:
                            return
                        if tile < NB:
                            act.wait_ge(weighted_done, u + 1)
                            done(act.activation(br_hi[:, tile, :], pb[3][:, 0:TOK], ACT.Copy), branch_hi)
                        else:
                            k = tile - NB + 1
                            act.wait_ge(tile_read, k)
                            done(act.activation(t1[:, :], t2[:, :], ACT.Square), sub_sq)
                            act.wait_ge(sub_ms, k)
                            done(act.activation(t3[:, :], pb[3][:, 0:TOK], ACT.Sqrt, scale=1.0 / 128, bias=eps[:, 1:2]), sub_std)
                            act.wait_ge(sub_done, k)
                            done(act.activation(br_hi[:, tile - NB, :], t2[:, :], ACT.Copy), branch_hi)

                    def attention(mine):
                        prev = None
                        for un in mine:
                            w = 128 if un["c"] == 0 else TOK
                            for n, _ in un["sets"]:
                                act.wait_ge(max_done, n + 1)
                                if n >= 4:
                                    act.wait_ge(probs_t, set_unit[n - 4] + 1)
                                done(act.activation(pr[:, n % 4, 0:w], pb[n % 2][:, 0:w], ACT.Exp, scale=SCALE,
                                               bias=st[:, n % 4, 1:2], accum_out=st[:, n % 4, 2:3]), exp_done)
                            if prev:
                                finish(prev)
                            prev = un
                        finish(prev)

                    attention([un for un in units if un["tile"] < NB])
                    branch(0, sig)
                    attention([un for un in units if un["tile"] >= NB])
                    branch(1, sig)

                    act.wait_ge(cmix_ready, C_BLOCKS)
                    done(act.activation(cmix[:, 12, :], cmix[:, 12, :], ACT.Tanh), lora_act)
                    done(act.activation(cmix[:, 14, :], cmix[:, 14, :], ACT.Sigmoid), lora_act)
                    nl = len(LEVELS) - 1
                    for g in range(2 * NB):
                        j, d = g // 2, g % 2
                        if d == 0:
                            act.wait_ge(kk_raw, j + 1)
                            done(act.activation(zi[:, :], kk[:, :], ACT.Square), kk_sq)
                            act.wait_ge(kk_ms, j + 1)
                            done(act.activation(zx[:, :], pb[3][:, 0:TOK], ACT.Sqrt, bias=eps[:, 3:4]), kk_std)
                        act.wait_ge(lora_done, g + 1)
                        link(act.activation(sg[:, :], pb[0][:, 0:TOK], ACT.Sigmoid, bias=par[:, 135 + 4 * d + j:136 + 4 * d + j]))
                        done(act.activation(aa[:, :], pb[1][:, 0:TOK], ACT.Sigmoid, bias=par[:, 143 + 4 * d + j:144 + 4 * d + j]
                                       ), sg_done)
                        act.wait_ge(z_ready, g + 1)
                        link(act.activation(sg[:, :], zi[:, :], ACT.Exp, scale=-KAPPA))
                        link(act.activation(zx[:, :], zx[:, :], ACT.Exp, scale=-KAPPA))
                        link(act.activation(zi[:, :], zi[:, :], ACT.Exp, scale=KAPPA))
                        done(act.activation(eh[:, :], half[:, :], ACT.Exp, scale=-KAPPA), exps_done)
                        act.wait_ge(tok_t, g + 1)
                        link(act.activation(btok[:, :, :].rearrange("p c k -> p (c k)"), pb[0][:, 0:TOK], ACT.Copy))
                        done(act.activation(ktok[:, :, :].rearrange("p c k -> p (c k)"), pb[1][:, 0:TOK], ACT.Copy), tok_ready)
                        for f in range(6):
                            n = 6 * g + f
                            act.wait_ge(gram_done, n + 1)
                            done(act.activation(lt[:, 3 * (f % 2) + f // 2, :], pb[2 + n % 2][:, 0:128], ACT.Copy), lt_ready)
                        act.wait_ge(xi_t, g + 1)
                        link(act.activation(xi[:, 0:3, :].rearrange("p u s -> p (u s)"), pb[2][:, 0:TOK], ACT.Copy))
                        done(act.activation(xi[:, 3:6, :].rearrange("p u s -> p (u s)"), pb[3][:, 0:TOK], ACT.Copy), xi0_ready)
                        for n in range(1, nl + 1):
                            lv = nl * g + n
                            act.wait_ge(tl_done, lv)
                            done(act.activation(tl[:, :, :].rearrange("p u s -> p (u s)"), pb[0][:, 0:TOK], ACT.Copy), tl_ready)
                            act.wait_ge(xt_t, lv)
                            link(act.activation(xt[:, 0:3, :].rearrange("p u s -> p (u s)"), pb[2][:, 0:TOK], ACT.Copy))
                            done(act.activation(xt[:, 3:6, :].rearrange("p u s -> p (u s)"), pb[3][:, 0:TOK], ACT.Copy), xt_ready)
                        for i in range(3):
                            act.wait_ge(r_done, 3 * g + i + 1)
                            done(act.activation(rs[:, :], pb[0][:, 0:128], ACT.Copy), r_ready)
                            if i == 0:
                                act.wait_ge(spo_t, g + 1)
                                if g >= 1:
                                    act.wait_ge(st_out, 32 * g)
                                done(act.activation(spt[:, :], pb[3][:, 128:256], ACT.Copy), spo_ready)
                        if d == 1:
                            act.wait_ge(gn_centred, j + 1)
                            done(act.activation(zi[:, :], osum[:, :], ACT.Square), gn_sq)
                            act.wait_ge(gn_var, j + 1)
                            done(act.activation(zx[:, :], pb[2][:, 0:TOK], ACT.Sqrt, scale=1.0 / HD, bias=eps[:, 2:3]), gn_std)
                            act.wait_ge(out_done, j + 1)
                            done(act.activation(brc_hi[:, j, :], osum[:, :], ACT.Copy), brc_hi_s)
                    branch(2, sigc)
                    act.wait_ge(merged_done, NBR * KD)
                    for m in range(KD):
                        done(act.activation(xm_hi[:, m, :], merged[:, m, :], ACT.Copy), xhi_ready)
                    for m in range(KD):
                        ahead(("w", m))
                    layer_norm(1)
                    xm_high(2, 3)
                    ffn(1)
                    layer_norm(2)

                @block.gpsimd
                def _(pool):
                    link, done, freed = linker(pool, pch)

                    def scale_x(s, n):
                        pool.wait_ge(xm_ready, n)
                        xf = x[:, :, :].rearrange("p k t -> p (k t)")
                        done(pool.tensor_scalar(xf, xf, ALPHA, 1.0, ALU.mult, ALU.mult), scaled)

                    scale_x(0, KD)
                    pool.wait_ge(xm_ready, 2 * KD)
                    done(pool.memset(cin[:, :, :], 0.0), pads)
                    scale_x(1, 2 * KD)
                    for i in range(C_BLOCKS):
                        wait_freed(pool, ("c", i))
                        if i >= 2:
                            pool.wait_ge(cmix_ready, i - 1)
                        done(pool.tensor_tensor(csum[:, i % 2, :], cin[:, i % 3, 0:386], cin[:, i % 3, 2:388], ALU.add
                                           ), csum_ready)
                    pool.wait_ge(merged_done, 2 * KD)
                    pool.wait_ge(kv_out, 64)
                    link(pool.memset(sld[:, :], 0.0))
                    done(pool.memset(spo[:, :], 0.0), pads)
                    for g in range(2 * NB):
                        d = g % 2
                        for n in range(len(LEVELS)):
                            if n == 0:
                                pool.wait_ge(lt_ready, 6 * g + 6)
                                if g >= 1:
                                    pool.wait_ge(tl_done, 6 * g)
                            elif n == 1:
                                pool.wait_ge(xt0_ready, g + 1)
                            else:
                                pool.wait_ge(tl_done, 6 * g + n - 1)
                            o = CO_LEV + (d * len(LEVELS) + n) * 128
                            done(pool.tensor_tensor(ltm[:, :, :], lt[:, :, :], over(cst[:, o:o + 128], 6), ALU.mult
                                               ), ltm_ready)
                    scale_x(2, 4 * KD)

                @block.vector
                def _(dve):
                    link, done, freed = linker(dve, dch)
                    nsplit = [0]

                    def splits_to(n):
                        for c in range(nsplit[0], min(n + 1, NCHUNK)):
                            dve.wait_ge(hi_done, c + 1)
                            w = chunk_len(chunk_list[c])
                            done(dve.tensor_tensor(w_lo[:, c % SPL, 0:w], raw[:, c % RAW, 0:w],
                                              w_hi[:, c % SPL, 0:w].bitcast(F32), ALU.subtract), lo_done)
                            nsplit[0] = c + 1

                    def ahead(key):
                        splits_to(chunk_no[key] + LOOK)

                    def modulate(s, base):
                        def low(m):
                            dve.wait_ge(xhi_ready, KD * base + m + 1)
                            done(dve.tensor_tensor(xm_lo[:, m, :], sq[:, m % 4, :], xm_hi[:, m, :].bitcast(F32), ALU.subtract
                                              ), xm_ready)
                        for m in range(KD):
                            if s > 0:
                                dve.wait_ge(x_ready, KD * (s - 1) + m + 1)
                            for gi, (a, b) in enumerate(GROUPS):
                                ins = dve.tensor_scalar(sq[:, m % 4, a:b], x[:, m, a:b], modv[:, 3 * s + 1, m, gi:gi + 1],
                                                        modv[:, 3 * s, m, gi:gi + 1], ALU.mult, ALU.add)
                            done(ins, xf_ready)
                            if m >= 1:
                                low(m - 1)
                        low(KD - 1)

                    def residual(s, key, m):
                        wait_group(dve, key)
                        dve.wait_ge(scaled, s + 1)
                        for gi, (a, b) in enumerate(GROUPS):
                            ins = dve.scalar_tensor_tensor(out=x[:, m, a:b], in0=gbank(key)[:, a:b],
                                                           scalar=modv[:, 3 * s + 2, m, gi:gi + 1], in1=x[:, m, a:b],
                                                           op0=ALU.mult, op1=ALU.add)
                        freed(ins, key)

                    def layer_norm(s):
                        dve.wait_ge(mean_done, s + 1)
                        for m in range(KD):
                            done(dve.scalar_tensor_tensor(out=x[:, m, :], in0=pb[1][:, 0:TOK], scalar=-1.0 / D, in1=x[:, m, :],
                                                     op0=ALU.mult, op1=ALU.add), d_ready)
                        dve.wait_ge(std_done, s + 1)
                        link(dve.reciprocal(rstd[:, :], mean[:, :]))
                        for m in range(KD):
                            done(dve.tensor_tensor(x[:, m, :], x[:, m, :], rstd[:, :], ALU.mult), n_ready)

                    def h_low(f, j):
                        dve.wait_ge(hhi_done, NF * f + j + 1)
                        done(dve.tensor_tensor(h_lo[:, j, :], hf[:, j % 2, :], h_hi[:, j, :].bitcast(F32), ALU.subtract
                                          ), h_ready)

                    def ffn(f):
                        for j in range(NF):
                            ka, kb = ("a", f, j), ("b", f, j)
                            ahead(ka)
                            ahead(kb)
                            wait_freed(dve, ka)
                            wait_group(dve, kb)
                            freed(dve.tensor_tensor(hf[:, j % 2, :], sa[:, j % 2, :], gbank(kb)[:, 0:TOK], ALU.mult
                                              ), kb)
                            if j >= 1:
                                h_low(f, j - 1)
                        h_low(f, NF - 1)
                        if f == 0:
                            dve.wait_ge(mod_done, NMODC)
                            take_mod(2, N_MOD)
                        for m in range(KD):
                            for c in range(3):
                                ahead(("o", f, m, c))
                            residual(2 * f, ("o", f, m), m)
                        layer_norm(2 * f)

                    def take_mod(a, b):
                        n0, n1 = a * KD, b * KD
                        mv = modv[:, :, :, :].rearrange("p n k g -> p (n k) g")
                        for gi in range(2):
                            ins = dve.tensor_tensor(mv[:, n0:n1, gi], pb[0][:, 0:2 * NMODC].rearrange("p (n g) -> p n g", g=2)[:, n0:n1, gi],
                                                    par[:, n0:n1], ALU.add)
                            link(ins)
                        for i in range(a, b):
                            if i % 3 == 1:
                                link(dve.tensor_scalar(modv[:, i, :, :], modv[:, i, :, :], 1.0, None, ALU.add))
                            elif i in (2, 8):
                                link(dve.tensor_scalar(modv[:, i, :, :], modv[:, i, :, :], 0.5, None, ALU.mult))

                    def branch(br, sg_, gu_):
                        for mp in range(KD // 2):
                            ahead(("g", br, 2 * mp))
                            ahead(("g", br, 2 * mp + 1))
                            ahead(("u", br, mp))
                            for e in range(2):
                                m = 2 * mp + e
                                gk, uk = ("g", br, m), ("u", br, m)
                                wait_freed(dve, gk)
                                wait_group(dve, uk)
                                if br == 0:
                                    freed(dve.tensor_tensor(merged[:, m, :], sg_[:, e, :], gbank(uk)[:, 0:TOK], ALU.mult
                                                      ), uk)
                                    wait_freed(dve, uk)
                                    dve.nop().then_inc(merged_done, 1)
                                else:
                                    freed(dve.tensor_tensor(gu_[:, e, :], sg_[:, e, :], gbank(uk)[:, 0:TOK], ALU.mult
                                                      ), uk)
                                    wait_freed(dve, uk)
                                    done(dve.tensor_tensor(merged[:, m, :], merged[:, m, :], gu_[:, e, :], ALU.add
                                                      ), merged_done)

                    dve.wait_ge(par_t, 1)
                    link(dve.tensor_copy(par[:, 0:174], pb[3][:, 0:174]))
                    link(dve.tensor_scalar(small[:, 8:12], par[:, 155:159], -1.0, 1.0, ALU.mult, ALU.add))
                    dve.wait_ge(mod_done, mod_first)
                    take_mod(0, 2)
                    dve.nop().then_inc(mod_read, 1)
                    splits_to(LOOK - 1)
                    modulate(0, 0)
                    ffn(0)
                    modulate(1, 1)

                    for i in range(C_BLOCKS):
                        ahead(("c", i))
                        dve.wait_ge(csum_ready, i + 1)
                        mu = par[:, 120 + i:121 + i]
                        link(dve.scalar_tensor_tensor(out=csum[:, i % 2, :], in0=csum[:, i % 2, :], scalar=0.5,
                                                      in1=cin[:, i % 3, 1:387], op0=ALU.mult, op1=ALU.subtract))
                        link(dve.scalar_tensor_tensor(out=cmix[:, i, 0:TP], in0=csum[:, i % 2, 0:TP], scalar=mu,
                                                 in1=cin[:, i % 3, 1:1 + TP], op0=ALU.mult, op1=ALU.add))
                        done(dve.scalar_tensor_tensor(out=cmix[:, i, TP:TOK], in0=csum[:, i % 2, TP + 2:TOK + 2], scalar=mu,
                                                 in1=cin[:, i % 3, 3 + TP:3 + TOK], op0=ALU.mult, op1=ALU.add
                                                 ), cmix_ready)
                    for key in qk_keys:
                        ahead(key)
                    for n, key in enumerate(v_keys):
                        ahead(key)
                        wait_group(dve, key)
                        src = gbank(key)[:, 0:TOK].rearrange("p (c v) -> p c v", c=NCH)
                        dst = va[:, 0:NCH, :] if n == 0 else vb[:, 0:NCH, (n - 1) * 128:n * 128]
                        freed(dve.tensor_copy(dst, src), key)
                    dve.wait_ge(lam_b, 1)
                    link(dve.tensor_copy(t2[:, 0:256], pb[3][:, 0:256]))
                    link(dve.tensor_tensor_reduce(t3[:, 0:64], t2[:, 0:64], t2[:, 64:128], 1.0, 0.0, ALU.mult, ALU.add, lam[:, 0:1]))
                    done(dve.tensor_tensor_reduce(t3[:, 64:128], t2[:, 128:192], t2[:, 192:256], 1.0, 0.0, ALU.mult, ALU.add,
                                             lam[:, 1:2]), lam_dot)
                    dve.wait_ge(lam_exp, 1)
                    link(dve.tensor_tensor(lam[:, 4:5], lam[:, 2:3], lam[:, 3:4], ALU.subtract))
                    link(dve.tensor_tensor(lam[:, 5:6], lam[:, 4:5], small[:, 0:1], ALU.add))
                    link(dve.tensor_scalar(lam[:, 6:7], lam[:, 5:6], -1.0, None, ALU.mult))
                    link(dve.tensor_tensor(small[:, 4:5], par[:, 171:172], small[:, 1:2], ALU.mult))
                    dve.wait_ge(kt_done, 1)
                    done(dve.tensor_copy(kc[:, 0:4, :].rearrange("p i t -> p (i t)"), pb[0][:, 0:512]), kc_ready)
                    dve.wait_ge(kt_done, 2)
                    done(dve.tensor_copy(kc[:, 4, :], pb[0][:, 0:128]), kc_ready)
                    for i in range(5):
                        dve.wait_ge(qstd_done, i + 1)
                        link(dve.reciprocal(t3[:, :], t2[:, :]))
                        gq = par[:, 172:173] if i < 4 else par[:, 173:174]
                        done(dve.scalar_tensor_tensor(out=qk[:, i, :], in0=qk[:, i, :], scalar=gq, in1=t3[:, :],
                                                 op0=ALU.mult, op1=ALU.mult), qn_ready)
                    for i in range(13):
                        dve.wait_ge(rot_done, i + 1)
                        link(dve.tensor_tensor(t2[:, 0:TS], cst[:, CO_SIN:CO_SIN + TS], pb[2 + i % 2][:, 0:TS], ALU.mult))
                        link(dve.tensor_tensor(t3[:, 0:TS], qk[:, i, TP:TOK], cst[:, CO_COS:CO_COS + TS], ALU.mult))
                        done(dve.tensor_tensor(qk[:, i, TP:TOK], t2[:, 0:TS], t3[:, 0:TS], ALU.add), rope_ready)
                    dve.wait_ge(swap_done, 1)
                    done(dve.tensor_copy(kswap[:, :], pb[0][:, :]), swap_ready)
                    dve.wait_ge(kout_t, 1)
                    done(dve.tensor_copy(kst[:, 0:4, :].rearrange("p i t -> p (i t)"), pb[1][:, 0:512]), kout_ready)
                    dve.wait_ge(kout_t, 2)
                    done(dve.tensor_copy(kst[:, 4, :], pb[1][:, 0:128]), kout_ready)

                    def finish(un):
                        u, tile = un["u"], un["tile"]
                        w = 128 if un["c"] == 0 else TOK
                        for n, e in un["sets"]:
                            s, p = n % 4, pr[:, n % 4, 0:w]
                            dve.wait_ge(exp_done, n + 1)
                            link(dve.reciprocal(st[:, s, 3:4], st[:, s, 2:3]))
                            if tile < NB:
                                done(dve.tensor_scalar(p, p, st[:, s, 3:4], None, ALU.mult), probs_ready)
                            elif e == 0:
                                link(dve.tensor_scalar(p, p, st[:, s, 3:4], None, ALU.mult))
                            else:
                                link(dve.tensor_tensor(st[:, s, 3:4], st[:, s, 3:4], lam[:, 6:7], ALU.mult))
                                done(dve.scalar_tensor_tensor(out=p, in0=p, scalar=st[:, s, 3:4], in1=pr[:, (n - 1) % 4, 0:w],
                                                         op0=ALU.mult, op1=ALU.add), probs_ready)
                        if not un["last"]:
                            return
                        if tile < NB:
                            dve.wait_ge(branch_hi, tile + 1)
                            done(dve.scalar_tensor_tensor(out=br_lo[:, tile, :], in0=pb[3][:, 0:TOK], scalar=1.0,
                                                     in1=br_hi[:, tile, :].bitcast(F32), op0=ALU.mult, op1=ALU.subtract
                                                     ), branch_ready)
                        else:
                            k = tile - NB + 1
                            dve.wait_ge(weighted_done, u + 1)
                            done(dve.tensor_copy(t2[:, :], pb[3][:, 0:TOK]), tile_read)
                            dve.wait_ge(sub_std, k)
                            link(dve.reciprocal(t3[:, :], t3[:, :]))
                            done(dve.scalar_tensor_tensor(out=t2[:, :], in0=t2[:, :], scalar=small[:, 4:5], in1=t3[:, :],
                                                     op0=ALU.mult, op1=ALU.mult), sub_done)
                            dve.wait_ge(branch_hi, tile + 1)
                            done(dve.tensor_tensor(br_lo[:, tile - NB, :], t2[:, :], br_hi[:, tile - NB, :].bitcast(F32),
                                              ALU.subtract), branch_ready)

                    def attention(mine):
                        prev = None
                        for un in mine:
                            w = 128 if un["c"] == 0 else TOK
                            for n, _ in un["sets"]:
                                dve.wait_ge(scored, n + 1)
                                link(dve.reduce_max(st[:, n % 4, 0:1], pb[n % 2][:, 0:w], AX_X))
                                done(dve.tensor_scalar(st[:, n % 4, 1:2], st[:, n % 4, 0:1], -SCALE, None, ALU.mult), max_done)
                            if prev:
                                finish(prev)
                            prev = un
                        finish(prev)

                    attention([un for un in units if un["tile"] < NB])
                    branch(0, sig, gu)
                    attention([un for un in units if un["tile"] >= NB])
                    branch(1, sig, gu)

                    dve.wait_ge(kv_out, 64)
                    for c in range(NCH):
                        dve.wait_ge(vtok_t, c + 1)
                        done(dve.tensor_copy(vtok[:, c, :], pb[c][:, :]), vtok_ready)
                    nl = len(LEVELS) - 1

                    def chunked(t):
                        return t[:, :].rearrange("p (c t) -> p c t", c=NCH)

                    for g in range(2 * NB):
                        j, d = g // 2, g % 2
                        r_, k_, v_ = cmix[:, j, :], cmix[:, 4 + j, :], cmix[:, 8 + j, :]
                        if d == 0:
                            done(dve.tensor_scalar(kk[:, :], k_, par[:, 151 + j:152 + j], None, ALU.mult), kk_raw)
                            dve.wait_ge(kk_std, j + 1)
                            link(dve.reciprocal(zx[:, :], zx[:, :]))
                            link(dve.tensor_tensor(kk[:, :], kk[:, :], zx[:, :], ALU.mult))
                        dve.wait_ge(sg_done, g + 1)
                        for c in range(NCH):
                            t = slice(c * 128, (c + 1) * 128)
                            ins = dve.tensor_tensor_scan(cs[:, t], ones, sg[:, t], 0.0, ALU.mult, ALU.add)
                        link(ins)
                        link(dve.tensor_scalar(half[:, :], chunked(cs)[:, :, 127], 0.5, None, ALU.mult))
                        for c in range(NCH):
                            t = slice(c * 128, (c + 1) * 128)
                            if d == 0:
                                ins = dve.tensor_scalar(zi[:, t], cs[:, t], half[:, c:c + 1], None, ALU.subtract)
                            else:
                                ins = dve.tensor_scalar(zx[:, t], cs[:, t], -1.0, half[:, c:c + 1], ALU.mult, ALU.add)
                        link(ins)
                        if d == 0:
                            done(dve.tensor_tensor(zx[:, :], zi[:, :], sg[:, :], ALU.subtract), z_ready)
                        else:
                            done(dve.tensor_tensor(zi[:, :], zx[:, :], sg[:, :], ALU.add), z_ready)
                        link(dve.tensor_scalar(cs[:, :], aa[:, :], par[:, 155 + j:156 + j], small[:, 8 + j:9 + j], ALU.mult, ALU.add))
                        link(dve.tensor_tensor(kt[:, :], cs[:, :], k_, ALU.mult))
                        if d == 0:
                            link(dve.tensor_copy(ksum[:, :], kt[:, :]))
                        else:
                            link(dve.tensor_tensor(ksum[:, :], ksum[:, :], kt[:, :], ALU.add))
                        link(dve.tensor_tensor(aa[:, :], aa[:, :], kk[:, :], ALU.mult))
                        dve.wait_ge(exps_done, g + 1)
                        link(dve.scalar_tensor_tensor(out=ar[:, :, 0, :], in0=chunked(kk), scalar=-1.0, in1=chunked(zx),
                                                 op0=ALU.mult, op1=ALU.mult))
                        link(dve.tensor_tensor(ar[:, :, 1, :], r_.rearrange("p (c t) -> p c t", c=NCH), chunked(sg), ALU.mult))
                        link(dve.tensor_tensor(bt[:, :], aa[:, :], zi[:, :], ALU.mult))
                        done(dve.tensor_tensor(kt[:, :], kt[:, :], zi[:, :], ALU.mult), ab_ready)
                        for f in range(6):
                            n = 6 * g + f
                            dve.wait_ge(lt_ready, n + 1)
                            u = 3 * (f % 2) + f // 2
                            src = pb[2 + n % 2][:, :].rearrange("p (i a t) -> p i a t", i=2, a=2)
                            link(dve.tensor_tensor(lak[:, u, :], src[:, 1, 0, :],
                                              cst[:, CO_STR + 128 * d:CO_STR + 128 * d + 128], ALU.mult))
                            done(dve.tensor_tensor(rbk[:, u, :, :], src[:, :, 1, :],
                                              over(cst[:, CO_INC + 128 * d:CO_INC + 128 * d + 128], 2), ALU.mult
                                              ), gram_read)
                        dve.wait_ge(ltm_ready, len(LEVELS) * g + 1)
                        done(dve.tensor_tensor(xt[:, :, :], ltm[:, :, :], over(ident, 6), ALU.add), xt0_ready)
                        for n in range(1, nl + 1):
                            b = LEVELS[n]
                            dve.wait_ge(u_done, nl * g + n)
                            cols = xi[:, :, :].rearrange("p u (q h b) -> p (u q) h b", h=2, b=b)[:, :, d, :]
                            done(dve.tensor_tensor(cols, cols, pb[1][:, 0:TOK].rearrange("p (q b) -> p q b", b=b), ALU.add
                                              ), xi_ready)
                        order = (0, 1, 2) if d == 0 else (0, 2, 1)
                        dve.wait_ge(state_t, g + 1)
                        c1, c2 = order[1], order[2]
                        done(dve.tensor_scalar(sp[:, :], pb[3][:, 0:128], eh[:, c1:c1 + 1], None, ALU.mult), sp_ready)
                        for i, c in enumerate(order):
                            n = 3 * g + i
                            dve.wait_ge(sa_done, n + 1)
                            done(dve.tensor_copy(sas[:, :], pb[1][:, 0:128]), sa_ready)
                            dve.wait_ge(o_done, n + 1)
                            t = slice(c * 128, (c + 1) * 128)
                            if d == 0:
                                done(dve.tensor_copy(osum[:, t], pb[2][:, 0:128]), o_read)
                            else:
                                done(dve.tensor_tensor(osum[:, t], osum[:, t], pb[2][:, 0:128], ALU.add), o_read)
                            if i < 2:
                                dve.wait_ge(sn_done, 2 * g + i + 1)
                                for hh in range(2):
                                    hs = slice(64 * hh, 64 * hh + 64)
                                    if i == 0:
                                        ins = dve.tensor_scalar(spo[hs, hs], pb[3][hs, hs], eh[hs, 0:1], None, ALU.mult)
                                    else:
                                        ins = dve.tensor_tensor(sp[hs, hs], sp[hs, hs], pb[3][hs, hs], ALU.add)
                                if i == 0:
                                    done(ins, sn_read)
                                else:
                                    link(ins)
                                    done(dve.tensor_scalar(sp[:, :], sp[:, :], eh[:, c1:c1 + 1], eh[:, c2:c2 + 1],
                                                      ALU.mult, ALU.mult), sp_ready)
                        if d == 1:
                            dve.wait_ge(gn_mean, j + 1)
                            done(dve.scalar_tensor_tensor(out=osum[:, :], in0=pb[1][:, 0:TOK], scalar=-1.0 / HD, in1=osum[:, :],
                                                     op0=ALU.mult, op1=ALU.add), gn_centred)
                            done(dve.scalar_tensor_tensor(out=cs[:, :], in0=r_, scalar=par[:, 159 + j:160 + j], in1=ksum[:, :],
                                                     op0=ALU.mult, op1=ALU.mult), bonus_in)
                            dve.wait_ge(gn_std, j + 1)
                            link(dve.reciprocal(zx[:, :], zx[:, :]))
                            link(dve.tensor_tensor(osum[:, :], osum[:, :], zx[:, :], ALU.mult))
                            link(dve.tensor_scalar(osum[:, :], osum[:, :], par[:, 163 + j:164 + j], par[:, 167 + j:168 + j],
                                                   ALU.mult, ALU.add))
                            dve.wait_ge(bonus_sum, j + 1)
                            link(dve.tensor_tensor(cs[:, :], v_, pb[3][:, 0:TOK], ALU.mult))
                            link(dve.tensor_tensor(osum[:, :], osum[:, :], cs[:, :], ALU.add))
                            dve.wait_ge(out_gate, j + 1)
                            done(dve.tensor_tensor(osum[:, :], osum[:, :], pb[0][:, 0:TOK], ALU.mult), out_done)
                            dve.wait_ge(brc_hi_s, j + 1)
                            done(dve.tensor_tensor(brc_lo[:, j, :], osum[:, :], brc_hi[:, j, :].bitcast(F32), ALU.subtract
                                              ), brc_ready)
                    branch(2, sigc, guc)
                    for m in range(KD):
                        dve.wait_ge(xhi_ready, 2 * KD + m + 1)
                        done(dve.tensor_tensor(xm_lo[:, m, :], merged[:, m, :], xm_hi[:, m, :].bitcast(F32), ALU.subtract
                                          ), xm_ready)
                    for m in range(KD):
                        ahead(("w", m))
                        residual(1, ("w", m), m)
                    layer_norm(1)
                    modulate(2, 3)
                    ffn(1)
            nc.multi_engine_barrier([e.engine for e in (nc.sync, nc.scalar, nc.vector, nc.tensor, nc.gpsimd)],
                                    sems_to_clear=range(sems[0].num, sems[-1].num + 1))

        with nc.Block() as block:
            @block.tensor
            def _(pe):
                for c in range(NCH):
                    for hf_ in range(2):
                        n = 2 * c + hf_
                        if n >= 4:
                            pe.wait_ge(fin_cp, n - 3)
                        for k in range(4):
                            mm = pe.transpose(pb[n % 4][:, k * 128:(k + 1) * 128], x[:, 4 * hf_ + k, c * 128:(c + 1) * 128], ident)
                        mm.then_inc(fin_t, 1)

            @block.vector
            def _(dve):
                for n in range(2 * NCH):
                    dve.wait_ge(fin_t, n + 1)
                    dve.tensor_copy(xrows[:, n // 2, (n % 2) * 512:(n % 2) * 512 + 512], pb[n % 4][:, :]).then_inc(fin_cp, 1)

            @block.sync
            def _(sy):
                sy.wait_ge(fin_cp, 2)
                sy.dma_start(O["y_prompt"][0], xrows[:, 0, :]).then_inc(y_out, 16)
                sy.wait_ge(fin_cp, 2 * NCH)
                sy.dma_start(O["y_sample"][0].rearrange("(c p) d -> p c d", p=128), xrows[:, 1:3, :]).then_inc(y_out, 16)
                sy.wait_ge(y_out, 32)


_OUTS = {"y_prompt": (1, TP, D), "y_sample": (1, TS, D), "new_attn_k": (1, DEPTH, 2, TP, HD), "new_attn_v": (1, DEPTH, 2, TP, HD),
         "new_diff_k": (1, DEPTH, 4, TP, 128), "new_diff_v": (1, DEPTH, 4, TP, 128),
         "new_state": (1, DEPTH, 2, 8, HD, HD)}
_LAYER_VIEWS = {"cache_attn_k": "cache_attn_k_l", "cache_attn_v": "cache_attn_v_l", "cache_diff_k": "cache_diff_k_l",
                "cache_diff_v": "cache_diff_v_l", "state_rwkv": "state_rwkv_l"}


def kernel(**inputs):
    import numpy as _np
    import concourse.bacc as _bacc
    from concourse import mybir as _mybir
    from concourse.bass_utils import run_bass_kernel_spmd as _run

    nc = _bacc.Bacc("TRN2", target_bir_lowering=False, num_devices=1)
    arrays, I, O = {}, {}, {}
    for name, a in dict(inputs, const=shape_constants()).items():
        a = _np.ascontiguousarray(a)
        arrays[f"in_{name}"] = a
        I[name] = nc.dram_tensor(f"in_{name}", a.shape, _mybir.dt.from_np(a.dtype), kind="ExternalInput").ap()
        if name in _LAYER_VIEWS:
            I[_LAYER_VIEWS[name]] = I[name][0]
    for name, shape in _OUTS.items():
        O[name] = nc.dram_tensor(f"out_{name}", shape, _mybir.dt.float32, kind="ExternalOutput").ap()
        O[name + "_l"] = O[name][0]
    build(nc, I, O)
    r = _run(nc, [arrays], core_ids=[0])
    return tuple(r.results[0][f"out_{name}"] for name in _OUTS)
```

```python
import math
from contextlib import ExitStack

import numpy as np

import concourse.bass as bass
from concourse import mybir

ALU = mybir.AluOpType
ACT = mybir.ActivationFunctionType
AX_X = mybir.AxisListType.X
F32 = mybir.dt.float32
F32R = mybir.dt.float32r

D = 1024
KD = D // 128
DEPTH = 2
TP = 128
TS = 256
TOK = TP + TS
NCH = TOK // 128
PAST = 128
HD = 64
F = 2816
NF = F // 128
FH = 8
NBR = 3
N_MOD = 9
BW = 512
NB = BW // 128
GRID_W = 64
ALPHA = (2.0 * DEPTH) ** 0.25
LN_EPS = 1e-5
RMS_EPS = 1e-6
GN_EPS = 64e-5
KAPPA = math.exp(-0.5)
SCALE = HD ** -0.5
C_BLOCKS = 15
GROUPS = ((0, TP), (TP, TOK))
COL_AQ, COL_AK, COL_AV = 3072, 3584, 3712
COL_BQ, COL_BK, COL_BV, COL_C = 3840, 4352, 4864, 5376
LEVELS = (1, 2, 4, 8, 16, 32, 64)
NL = len(LEVELS) - 1
B_QK = [(kind, i) for kind in ("bq", "bk") for i in range(4)]
V_KEYS = [("av", 0)] + [("bv", i) for i in range(4)]
ACC = 4
RAW, SPL, LOOK = 3, 4, 2
MODR = 7

CO_ID, CO_ONE, CO_BLK, CO_ROT, CO_SWAP = 0, 128, 256, 384, 512
CO_COS = 640
CO_SIN = CO_COS + TS
CO_LEV = CO_SIN + TS
CO_STR = CO_LEV + 2 * len(LEVELS) * 128
CO_INC = CO_STR + 256
CO_LAM = CO_INC + 256
CO_N = CO_LAM + 2 * DEPTH


def shape_constants():
    c = np.zeros((128, CO_N), np.float32)
    i = np.arange(128)
    c[:, CO_ID:CO_ID + 128] = np.eye(128)
    c[:, CO_ONE:CO_ONE + 128] = 1.0
    c[:, CO_BLK:CO_BLK + 128] = (i[:, None] // HD == i[None] // HD)
    for m in range(128):
        first = m % 32 < 16
        c[m + 16 if first else m - 16, CO_ROT + m] = -1.0 if first else 1.0
        c[(m + HD) % 128, CO_SWAP + m] = 1.0
    t = np.arange(TS)
    row, col = (t // GRID_W).astype(np.float32), (t % GRID_W).astype(np.float32)
    inv = (1.0 / (np.float32(10000.0) ** (np.arange(0, 32, 2, dtype=np.float32) / np.float32(32)))).astype(np.float32)
    for p in range(128):
        axis, f = (p % HD) // 32, p % 16
        ang = (row if axis == 0 else col) * inv[f]
        c[p, CO_COS:CO_COS + TS] = np.cos(ang)
        c[p, CO_SIN:CO_SIN + TS] = np.sin(ang)
    s, t = i[:, None], i[None]
    for d in range(2):
        a, b = (s, t) if d == 0 else (t, s)
        for n, size in enumerate(LEVELS):
            m = (a // (2 * size) == b // (2 * size)) & (a // size % 2 == 0) & (b // size % 2 == 1)
            o = CO_LEV + (d * len(LEVELS) + n) * 128
            c[:, o:o + 128] = m
        c[:, CO_STR + d * 128:CO_STR + d * 128 + 128] = a < b
        c[:, CO_INC + d * 128:CO_INC + d * 128 + 128] = a <= b
    for l in range(DEPTH):
        lam_init = 0.8 - 0.6 * math.exp(-0.3 * l)
        c[:, CO_LAM + 2 * l] = lam_init
        c[:, CO_LAM + 2 * l + 1] = 1.0 - lam_init
    return c


def plan_fillers():
    fill = [[] for _ in range(3 * NB * NCH)]
    b0 = 2 * NB * NCH
    for i in range(NB):
        fill[i].append(("bv", i))
        fill[i + 1].insert(0, ("vt", i + 1))
    for m in range(KD):
        fill[NB + m] += [("rot", 5 + m), ("g", 0, m)]
        fill[NB + KD + m].append(("g", 1, m))
        fill[b0 if m == 0 else b0 + 2 + m].append(("g", 2, m))
    for mp in range(KD // 2):
        fill[b0 + 1 + mp // 2].append(("u", 0, mp))
    return fill


def plan_layer():
    chunks, groups, last = [], [], {}

    def ffn(f):
        for j in range(NF):
            for part in "ab":
                chunks.append((part, f, j))
                groups.append((part, f, j))
        for m in range(KD):
            chunks.extend(("o", f, m, c) for c in range(3))
            groups.append(("o", f, m))

    def one(*key):
        chunks.append(key)
        groups.append(key)

    def up(br, mp):
        chunks.append(("u", br, mp))
        groups.append(("u", br, 2 * mp))
        groups.append(("u", br, 2 * mp + 1))

    ffn(0)
    for i in range(C_BLOCKS):
        one("c", i)
    for i in range(4):
        one("aq", i)
    one("ak", 0)
    one("av", 0)
    groups.append(("vt", 0))
    for key in B_QK:
        one(*key)
    for unit in plan_fillers():
        for key in unit:
            if key[0] in ("rot", "vt"):
                groups.append(key)
            elif key[0] == "u":
                up(*key[1:])
            else:
                one(*key)
    for br in (1, 2):
        for mp in range(KD // 2):
            up(br, mp)
    for m in range(KD):
        one("w", m)
    ffn(1)
    chunk_no = {k: n for n, k in enumerate(chunks)}
    for g in groups:
        if g[0] in ("rot", "vt"):
            continue
        last[g] = chunk_no[(g + (2,)) if g[0] == "o" else ("u", g[1], g[2] // 2) if g[0] == "u" else g]
    return chunk_no, {k: n for n, k in enumerate(groups)}, last


def plan_attention():
    units, n = [], 0
    for tile in range(2 * NB):
        mine = []
        for c in range(NCH):
            if tile < NB:
                for e in range(2):
                    mine.append({"c": c, "e": e, "sets": [(n, e)]})
                    n += 1
            else:
                mine.append({"c": c, "e": 0, "sets": [(n, 0), (n + 1, 1)]})
                n += 2
        for i, un in enumerate(mine):
            un.update(tile=tile, first=i == 0, last=i == len(mine) - 1, u=len(units))
            units.append(un)
    owner = {sn: un["u"] for un in units for sn, _ in un["sets"]}
    return units, owner


def scan_order(g):
    return (0, 1, 2) if g % 2 == 0 else (0, 2, 1)


def mod_schedule():
    total = N_MOD * KD
    steps = 2 * NF
    first = 2 * KD
    return first, [min(total, first + -(-(total - first) * (i + 1) // steps)) for i in range(steps)]


def build(nc, I, O):
    chunk_no, group_no, group_end = plan_layer()
    units, set_unit = plan_attention()
    chunk_list = list(chunk_no)
    NCHUNK = len(chunk_list)
    mod_first, mod_after = mod_schedule()
    fillers = plan_fillers()
    NMODC = N_MOD * KD
    qk_keys = [("aq", i) for i in range(4)] + [("ak", 0)] + B_QK

    def over(ap, n):
        return ap.rearrange("p (o w) -> p o w", o=1).to_broadcast([128, n, ap.shape[1]])

    glob = ExitStack()
    with glob:
        def sb(name, shape, dt=F32, ctx=glob):
            return ctx.enter_context(nc.sbuf_tensor(name, shape, dt))

        def sem(name):
            sems.append(glob.enter_context(nc.semaphore(name)))
            return sems[-1]

        sems = []

        cst = sb("cst", [128, CO_N])
        x = sb("x", [128, KD, TOK])
        xm_hi = sb("xm_hi", [128, KD, TOK], F32R)
        with ExitStack() as same:
            xm_lo = sb("xm_lo", [128, KD, TOK], F32R, same)
        rbk = sb("rbk", [128, 2, 6, 2, 128])
        raw = sb("raw", [128, RAW, 1024])
        spare = (chunk_no[("u", 2, 0)] + LOOK) % SPL
        with ExitStack() as same:
            w_hi = sb("w_hi", [128, SPL, 1024], F32R, same)
        if spare > 0:
            sb("w_hi_before", [128, spare, 1024])
        lt_odd = sb("lt_odd", [128, 6, 128])
        rs, sas = sb("rs", [128, 128]), sb("sas", [128, 128])
        if spare < SPL - 1:
            sb("w_hi_after", [128, (SPL - 1 - spare) * 1024])
        with ExitStack() as same:
            w_lo = sb("w_lo", [128, SPL, 1024], F32R, same)
        if spare > 0:
            sb("w_lo_before", [128, spare, 1024])
        bt, kt = sb("bt", [128, TOK]), sb("kt", [128, TOK])
        sp, spt = sb("sp", [128, 128]), sb("spt", [128, 128])
        if spare < SPL - 1:
            sb("w_lo_after", [128, (SPL - 1 - spare) * 1024])
        par = sb("par", [128, 176])
        modv = sb("modv", [128, N_MOD, KD, 2])
        condT = sb("condT", [128, KD, 2])
        lam = sb("lam", [128, 8])
        small = sb("small", [128, 16])
        eps = sb("eps", [128, 4])
        ident = cst[:, CO_ID:CO_ID + 128]
        ones = cst[:, CO_ONE:CO_ONE + 128]
        blk = cst[:, CO_BLK:CO_BLK + 128]

        with ExitStack() as ph:
            h_hi = sb("h_hi", [128, NF, TOK], F32R, ph)
            h_lo = sb("h_lo", [128, NF, TOK], F32R, ph)
            modw = sb("modw", [128, MODR, 1024], ctx=ph)
            sa = sb("sa", [128, 2, TOK], ctx=ph)
            hf = sb("hf", [128, 2, TOK], ctx=ph)
            pst = sb("pst", [128, 2, 128], ctx=ph)
            mrow = sb("mrow", [2, 2, 512], ctx=ph)
        with ExitStack() as ph:
            sq = sb("sq", [128, 4, TOK], ctx=ph)
            mean = sb("mean", [128, TOK], ctx=ph)
            rstd = sb("rstd", [128, TOK], ctx=ph)
            xrows = sb("xrows", [128, NCH, D], ctx=ph)
        with ExitStack() as mix:
            cmix = sb("cmix", [128, C_BLOCKS, TOK], ctx=mix)
            merged = sb("merged", [128, KD, TOK], ctx=mix)
            with ExitStack() as ph:
                with ExitStack() as same:
                    gate2 = sb("gate2", [128, KD, TOK], ctx=same)
                kst = sb("kst", [128, 5, 128], ctx=ph)
                kswap = sb("kswap", [128, TOK + PAST], ctx=ph)
                qk = sb("qk", [128, 13, TOK], ctx=ph)
                gate1 = sb("gate1", [128, KD, TOK], ctx=ph)
                br_hi = sb("br_hi", [128, NB, TOK], F32R, ph)
                br_lo = sb("br_lo", [128, NB, TOK], F32R, ph)
                gu = sb("gu", [128, 2, TOK], ctx=ph)
                with ExitStack() as same:
                    cin = sb("cin", [128, 3, 388], ctx=same)
                    csum = sb("csum", [128, 2, 386], ctx=same)
                pr = sb("pr", [128, 4, TOK], ctx=ph)
                pT = sb("pT", [128, 2, 3, 128], ctx=ph)
                kc = sb("kc", [128, 5, PAST], ctx=ph)
                va = sb("va", [128, 4, 128], ctx=ph)
                vb = sb("vb", [128, 4, 512], ctx=ph)
                rt = gu[:, :, 0:TS]
                t1 = sb("t1", [128, TOK], ctx=ph)
                t2 = sb("t2", [128, TOK], ctx=ph)
                t3 = sb("t3", [128, TOK], ctx=ph)
                st = sb("st", [128, 4, 4], ctx=ph)
            with ExitStack() as ph:
                sb("gate2_kept", [128, KD, TOK], ctx=ph)
                guc = sb("guc", [128, 2, TOK], ctx=ph)
                lora_w = sb("lora_w", [128, BW], ctx=ph)
                lora_a = sb("lora_a", [128, BW], ctx=ph)
                lora_g = sb("lora_g", [128, BW], ctx=ph)
                vtok = sb("vtok", [128, NCH, BW], ctx=ph)
                kk = sb("kk", [128, TOK], ctx=ph)
                osum = sb("osum", [128, TOK], ctx=ph)
                ksum = sb("ksum", [128, 2, TOK], ctx=ph)
                sg = sb("sg", [128, TOK], ctx=ph)
                aa = sb("aa", [128, TOK], ctx=ph)
                cs = sb("cs", [128, TOK], ctx=ph)
                zi = sb("zi", [128, TOK], ctx=ph)
                zx = sb("zx", [128, TOK], ctx=ph)
                half = sb("half", [128, NCH], ctx=ph)
                eh = sb("eh", [128, 2, NCH], ctx=ph)
                ar = sb("ar", [128, 2, NCH, 2, 128], ctx=ph)
                btok = sb("btok", [128, 2, NCH, 128], ctx=ph)
                ktok = sb("ktok", [128, 2, NCH, 128], ctx=ph)
                lak = sb("lak", [128, 2, 6, 128], ctx=ph)
                xt = sb("xt", [128, 2, 6, 128], ctx=ph)
                lt = (sb("lt_even", [128, 6, 128], ctx=ph), lt_odd)
                ltm = sb("ltm", [128, 6, 128], ctx=ph)
                xi = sb("xi", [128, 6, 128], ctx=ph)
                tl = sb("tl", [128, 6, 128], ctx=ph)
                sld = sb("sld", [128, 128], ctx=ph)
                spo = sb("spo", [128, 128], ctx=ph)
        brc_hi, brc_lo = xm_hi[:, 0:NB, :], xm_hi[:, NB:2 * NB, :]

        acc = [glob.enter_context(nc.psum_tensor(f"acc{i}", [128, 512], F32)) for i in range(ACC)]
        pb = [glob.enter_context(nc.psum_tensor(f"pb{i}", [128, 512], F32)) for i in range(4)]

        raw_in = [sem(f"raw_in{i}") for i in range(RAW)]
        hi_done, lo_done, chunk_used = sem("hi_done"), sem("lo_done"), sem("chunk_used")
        acc_free = [sem(f"acc_free{i}") for i in range(ACC)]
        mod_in = [sem(f"mod_in{i}") for i in range(MODR)]
        mod_done, mod_read = sem("mod_done"), sem("mod_read")
        mod_row, mod_t = sem("mod_row"), sem("mod_t")
        dch, ach, pch = sem("dve_chain"), sem("act_chain"), sem("pool_chain")
        par_in, par_t, par_done = sem("par_in"), sem("par_t"), sem("par_done")
        xf_ready, xhi_ready, xm_ready, scaled = sem("xf_ready"), sem("xhi_ready"), sem("xm_ready"), sem("scaled")
        silu_done, hhi_done, h_ready = sem("silu_done"), sem("hhi_done"), sem("h_ready")
        mean_done, d_ready, sq_ready, sq_used = sem("mean_done"), sem("d_ready"), sem("sq_ready"), sem("sq_used")
        std_done, n_ready, x_ready = sem("std_done"), sem("n_ready"), sem("x_ready")
        lam_in, lam_b, lam_dot, lam_exp, lam_done = (sem(n) for n in ("lam_in", "lam_b", "lam_dot", "lam_exp", "lam_done"))
        pads, cin_ready, csum_ready, cmix_ready = (sem(n) for n in ("pads", "cin_ready", "csum_ready", "cmix_ready"))
        qk_ready, qsq_ready, qms_done, qstd_done, qn_ready = (
            sem(n) for n in ("qk_ready", "qsq_ready", "qms_done", "qstd_done", "qn_ready"))
        rot_done, rope_ready, swap_done, swap_ready = (sem(n) for n in ("rot_done", "rope_ready", "swap_done", "swap_ready"))
        cache_in, kt_done, kc_ready = (sem(n) for n in ("cache_in", "kt_done", "kc_ready"))
        vt_done, kout_t, kout_ready, kv_out = (sem(n) for n in ("vt_done", "kout_t", "kout_ready", "kv_out"))
        scored, max_done, exp_done, probs_ready = (sem(n) for n in ("scored", "max_done", "exp_done", "probs_ready"))
        probs_t, probs_t_ready, weighted_done = (sem(n) for n in ("probs_t", "probs_t_ready", "weighted_done"))
        tile_read, branch_hi, branch_ready = (sem(n) for n in ("tile_read", "branch_hi", "branch_ready"))
        sub_sq, sub_ms, sub_std, sub_done = (sem(n) for n in ("sub_sq", "sub_ms", "sub_std", "sub_done"))
        sig_done, gated, merged_done, merged_hi = (sem(n) for n in ("sig_done", "gated", "merged_done", "merged_hi"))
        lora_in, lora_act, vtok_t, vtok_ready = (sem(n) for n in ("lora_in", "lora_act", "vtok_t", "vtok_ready"))
        kk_raw, kk_sq, kk_ms, kk_std, kk_ready = (sem(n) for n in ("kk_raw", "kk_sq", "kk_ms", "kk_std", "kk_ready"))
        lora_decay, decay_done, lora_done, sg_done, z_ready, exps_done, ab_ready = (
            sem(n) for n in ("lora_decay", "decay_done", "lora_rate", "sg_done", "z_ready", "exps_done", "ab_ready"))
        tok_t, tok_ready, gram_done, gram_read = (sem(n) for n in ("tok_t", "tok_ready", "gram_done", "gram_read"))
        lt_ready = sem("lt_ready")
        ltm_ready, xt0_ready, xt_ready, xi_t, xi0_ready, xi_ready = (
            sem(n) for n in ("ltm_ready", "xt0_ready", "xt_ready", "xi_t", "xi0_ready", "xi_ready"))
        tl_done, tl_ready, u_done, xt_t = (sem(n) for n in ("tl_done", "tl_ready", "u_done", "xt_t"))
        state_in, state_t, sp_ready = (sem(n) for n in ("state_in", "state_t", "sp_ready"))
        r_done, r_ready, sa_done, sa_ready = (sem(n) for n in ("r_done", "r_ready", "sa_done", "sa_ready"))
        o_done, o_read, sn_done, sn_read = (sem(n) for n in ("o_done", "o_read", "sn_done", "sn_read"))
        spo_t, spo_ready, st_out = (sem(n) for n in ("spo_t", "spo_ready", "st_out"))
        gn_mean, gn_centred, gn_sq, gn_var, gn_std = (sem(n) for n in ("gn_mean", "gn_centred", "gn_sq", "gn_var", "gn_std"))
        bonus_in, bonus_sum, bonus_read, out_gate, out_done = (
            sem(n) for n in ("bonus_in", "bonus_sum", "bonus_read", "out_gate", "out_done"))
        brc_hi_s, brc_ready = sem("brc_hi_done"), sem("brc_ready")
        init_in, init_t, init_done, fin_t, fin_cp, y_out = (
            sem(n) for n in ("init_in", "init_t", "init_done", "fin_t", "fin_cp", "y_out"))

        def linker(eng, chain):
            count = {}

            def done(ins, s):
                count[s.name] = count.get(s.name, 0) + 1
                ins.then_inc(s, 1)
                eng.wait_ge(s, count[s.name])

            def link(ins):
                done(ins, chain)

            def freed(ins, key):
                ins.then_inc(free_sem(key), 1)
                wait_freed(eng, key)
            return link, done, freed

        def gbank(key):
            return acc[group_no[key] % ACC]

        def wait_group(eng, key):
            eng.wait_ge(chunk_used, group_end[key] + 1)

        def free_sem(key):
            return acc_free[group_no[key] % ACC]

        def wait_freed(eng, key):
            eng.wait_ge(free_sem(key), group_no[key] // ACC + 1)

        with nc.Block() as block:
            @block.sync
            def _(sy):
                sy.dma_start(cst[:, :], I["const"]).then_inc(init_in, 16)
                sy.dma_start(xrows[:, 0, :], I["x_prompt"][0]).then_inc(init_in, 16)
                sy.dma_start(xrows[:, 1:3, :], I["x_sample"][0].rearrange("(c p) d -> p c d", p=128)).then_inc(init_in, 16)
                sy.dma_start(sq[0:KD, 0, 0:128], I["c_ctx"].rearrange("(k p) -> k p", p=128)).then_inc(init_in, 16)
                sy.dma_start(sq[0:KD, 0, 128:256], I["c"][0].rearrange("(k p) -> k p", p=128)).then_inc(init_in, 16)

            @block.tensor
            def _(pe):
                pe.wait_ge(init_in, 80)
                for k in range(KD):
                    if k >= 4:
                        pe.wait_ge(init_done, k - 3)
                    for c in range(NCH):
                        mm = pe.transpose(pb[k % 4][:, c * 128:(c + 1) * 128], xrows[:, c, k * 128:(k + 1) * 128], ident)
                    mm.then_inc(init_t, 1)
                for g in range(2):
                    mm = pe.transpose(acc[0][:, g * KD:(g + 1) * KD], sq[0:KD, 0, g * 128:(g + 1) * 128], ident[0:KD, 0:KD])
                mm.then_inc(init_t, 1)

            @block.vector
            def _(dve):
                for i, e in enumerate((LN_EPS, RMS_EPS, GN_EPS, 1e-12)):
                    dve.memset(eps[:, i:i + 1], e)
                for k in range(KD):
                    dve.wait_ge(init_t, k + 1)
                    dve.tensor_copy(x[:, k, :], pb[k % 4][:, 0:TOK]).then_inc(init_done, 1)

            @block.scalar
            def _(act):
                act.wait_ge(init_t, KD + 1)
                act.activation(condT[:, :, :].rearrange("p k g -> p g k"),
                               acc[0][:, 0:2 * KD].rearrange("p (g k) -> p g k", g=2), ACT.Silu)

        with nc.Fori(0, DEPTH) as l:
            def lay(name):
                ap = I[name]
                return ap[bass.ds(l, 1)]

            def chunk_src(key):
                kind = key[0]
                if kind in "ab" and len(kind) == 1:
                    _, f, j = key
                    c0 = (0 if kind == "a" else F) + j * 128
                    return lay("ffn_w_in")[:, f, :, c0:c0 + 128].rearrange("l (k p) c -> p (l k) c", p=128), KD, 128
                if kind == "o":
                    _, f, m, c = key
                    nk = min(FH, NF - FH * c)
                    r0 = c * FH * 128
                    return (lay("ffn_w_out")[:, f, r0:r0 + nk * 128, m * 128:(m + 1) * 128]
                            .rearrange("l (k p) c -> p (l k) c", p=128), nk, 128)
                if kind == "u":
                    _, br, mp = key
                    return lay("w_up")[:, br, :, mp * 256:(mp + 1) * 256].rearrange("l (k p) c -> p (l k) c", p=128), NB, 256
                if kind == "w":
                    return lay("w_out")[:, :, key[1] * 128:(key[1] + 1) * 128].rearrange("l (k p) c -> p (l k) c", p=128), KD, 128
                base = {"c": COL_C, "aq": COL_AQ, "ak": COL_AK, "av": COL_AV, "bq": COL_BQ, "bk": COL_BK, "bv": COL_BV}
                c0 = key[1] * D + key[2] * 128 if kind == "g" else base[kind] + key[1] * 128
                return lay("w_in")[:, :, c0:c0 + 128].rearrange("l (k p) c -> p (l k) c", p=128), KD, 128

            def chunk_len(key):
                return (min(FH, NF - FH * key[3]) * 128) if key[0] == "o" else 1024

            with nc.Block() as block:
                @block.sync
                def _(sy):
                    v = lambda n: lay(n)
                    rows = [(pst[0:72, 0, :], v("b_mod").rearrange("l (k p) -> (l k) p", p=128)),
                            (pst[72:96, 0, :], v("ln_g").rearrange("l s (k p) -> (l s k) p", p=128)),
                            (pst[96:120, 0, :], v("ln_b").rearrange("l s (k p) -> (l s k) p", p=128)),
                            (pst[0:15, 1, :], v("rwkv_mu").rearrange("l (k p) -> (l k) p", p=128)),
                            (pst[15:23, 1, :], v("rwkv_w0").rearrange("l s (k p) -> (l s k) p", p=128)),
                            (pst[23:31, 1, :], v("rwkv_a0").rearrange("l s (k p) -> (l s k) p", p=128)),
                            (pst[31:35, 1, :], v("rwkv_k_k").rearrange("l (k p) -> (l k) p", p=128)),
                            (pst[35:39, 1, :], v("rwkv_k_a").rearrange("l (k p) -> (l k) p", p=128)),
                            (pst[39:43, 1, :], v("rwkv_r_k").rearrange("l (k h) d -> (l k) (h d)", h=2)),
                            (pst[43:47, 1, :], v("rwkv_gn_g").rearrange("l (k p) -> (l k) p", p=128)),
                            (pst[47:51, 1, :], v("rwkv_gn_b").rearrange("l (k p) -> (l k) p", p=128)),
                            (pst[51:52, 1, :], v("diff_subln_g")),
                            (pst[52:54, 1, 0:HD], v("qk_norm_g").rearrange("l s d -> (l s) d")),
                            (pst[52:54, 1, HD:128], v("qk_norm_g").rearrange("l s d -> (l s) d"))]

                    def load_mod(q):
                        if q >= MODR:
                            sy.wait_ge(mod_done, q - MODR + 1)
                        sy.dma_start(modw[:, q % MODR, :].rearrange("p (k c) -> p k c", k=KD),
                                     lay("w_mod")[:, :, q * 128:(q + 1) * 128].rearrange("l (k p) c -> p (l k) c", p=128)
                                     ).then_inc(mod_in[q % MODR], 16)

                    def load_chunk(key):
                        n = chunk_no[key]
                        src, nk, nc_ = chunk_src(key)
                        if n >= RAW:
                            sy.wait_ge(lo_done, n - RAW + 1)
                        sy.dma_start(raw[:, n % RAW, 0:nk * nc_].rearrange("p (k c) -> p k c", k=nk), src
                                     ).then_inc(raw_in[n % RAW], 16)

                    for q in range(MODR):
                        load_mod(q)
                    for dst, src in rows:
                        sy.dma_start(dst, src).then_inc(par_in, 16)
                    for q in range(MODR, mod_first):
                        load_mod(q)
                    done = mod_first
                    for i in range(2 * NF):
                        load_chunk(("ab"[i % 2], 0, i // 2))
                        for q in range(done, mod_after[i]):
                            load_mod(q)
                        done = mod_after[i]
                    mid = chunk_no[("c", 0)]
                    for n in range(2 * NF, mid + LOOK):
                        load_chunk(chunk_list[n])
                    sy.dma_start(small[:, 0:2], I["const"][:, bass.ds(l * 2 + CO_LAM, 2)]).then_inc(lam_in, 16)
                    sy.wait_ge(xm_ready, 2 * KD)
                    sy.dma_start(kst[:, 0, :].rearrange("p (h d) -> p h d", h=2),
                                 lay("cache_attn_k_l").rearrange("l h p d -> p (l h) d")).then_inc(cache_in, 16)
                    sy.dma_start(kst[:, 1:5, :], lay("cache_diff_k_l").rearrange("l h p d -> p (l h) d")).then_inc(cache_in, 16)
                    sy.dma_start(va[:, 3, :].rearrange("p (h d) -> p h d", h=2),
                                 lay("cache_attn_v_l").rearrange("l h p d -> p (l h) d")).then_inc(cache_in, 16)
                    sy.dma_start(vb[:, 3, :].rearrange("p (h d) -> p h d", h=4),
                                 lay("cache_diff_v_l").rearrange("l h p d -> p (l h) d")).then_inc(cache_in, 16)
                    sy.dma_start(t3[0:1, 0:256], lay("diff_lambda").rearrange("l a d -> l (a d)")).then_inc(lam_in, 16)

                    stores = chunk_no[("g", 1, KD // 2)]
                    for n in range(mid + LOOK, stores):
                        load_chunk(chunk_list[n])
                    for n in range(NB + 1):
                        wait_freed(sy, ("vt", n))
                    sy.dma_start(O["new_attn_v_l"][bass.ds(l, 1)].rearrange("l h p d -> p (l h) d"),
                                 va[:, 0, :].rearrange("p (h d) -> p h d", h=2)).then_inc(kv_out, 16)
                    sy.dma_start(O["new_diff_v_l"][bass.ds(l, 1)].rearrange("l h p d -> p (l h) d"),
                                 vb[:, 0, :].rearrange("p (h d) -> p h d", h=4)).then_inc(kv_out, 16)
                    sy.wait_ge(kout_ready, 2)
                    sy.dma_start(O["new_attn_k_l"][bass.ds(l, 1)].rearrange("l h p d -> p (l h) d"),
                                 kst[:, 0, :].rearrange("p (h d) -> p h d", h=2)).then_inc(kv_out, 16)
                    sy.dma_start(O["new_diff_k_l"][bass.ds(l, 1)].rearrange("l h p d -> p (l h) d"),
                                 kst[:, 1:5, :]).then_inc(kv_out, 16)
                    rwk = chunk_no[("u", 2, 0)]
                    for n in range(stores, rwk + LOOK):
                        load_chunk(chunk_list[n])
                    sy.wait_ge(merged_done, KD)
                    sy.wait_ge(kv_out, 64)
                    sy.dma_start(lora_w[:, :], lay("rwkv_w2").rearrange("l s r c -> (l s r) c")).then_inc(lora_in, 16)
                    sy.dma_start(lora_a[:, :], lay("rwkv_a2").rearrange("l s r c -> (l s r) c")).then_inc(lora_in, 16)
                    sy.dma_start(lora_g[:, :], lay("rwkv_g2").rearrange("l r c -> (l r) c")).then_inc(lora_in, 16)
                    for n in range(rwk + LOOK, rwk + RAW):
                        load_chunk(chunk_list[n])
                    for g in range(2 * NB):
                        j, d = g // 2, g % 2
                        if g == 0:
                            sy.wait_ge(pads, 2)
                        else:
                            sy.wait_ge(state_t, g)
                        for hh in range(2):
                            sy.dma_start(sld[64 * hh:64 * hh + 64, 64 * hh:64 * hh + 64],
                                         lay("state_rwkv_l")[:, d, 2 * j + hh].rearrange("l v k -> (l v) k")
                                         ).then_inc(state_in, 16)
                        if g >= 1:
                            store_state = g - 1
                            jj, dd = store_state // 2, store_state % 2
                            sy.wait_ge(spo_ready, g)
                            for hh in range(2):
                                sy.dma_start(O["new_state_l"][bass.ds(l, 1), dd, 2 * jj + hh].rearrange("l v k -> (l v) k"),
                                             spt[64 * hh:64 * hh + 64, 64 * hh:64 * hh + 64]).then_inc(st_out, 16)
                    sy.wait_ge(spo_ready, 2 * NB)
                    for hh in range(2):
                        sy.dma_start(O["new_state_l"][bass.ds(l, 1), 1, 2 * (NB - 1) + hh].rearrange("l v k -> (l v) k"),
                                     spt[64 * hh:64 * hh + 64, 64 * hh:64 * hh + 64]).then_inc(st_out, 16)
                    for n in range(rwk + RAW, NCHUNK):
                        load_chunk(chunk_list[n])
                    sy.wait_ge(st_out, 16 * 4 * NB)

                @block.tensor
                def _(pe):
                    def open_group(key):
                        g = group_no[key]
                        if g >= ACC:
                            pe.wait_ge(acc_free[g % ACC], g // ACC)

                    def open_chunk(key):
                        pe.wait_ge(lo_done, chunk_no[key] + 1)

                    def weights(key, col):
                        s = chunk_no[key] % SPL
                        return w_hi[:, s, col:col + 128], w_lo[:, s, col:col + 128]

                    def mm3(out, lhs, rhs, first, last):
                        pe.matmul(out, lhs[0], rhs[0], start=first, stop=False)
                        pe.matmul(out, lhs[0], rhs[1], start=False, stop=False)
                        return pe.matmul(out, lhs[1], rhs[0], start=False, stop=last)

                    def xm_tile(k, t=slice(0, TOK)):
                        return xm_hi[:, k, t], xm_lo[:, k, t]

                    def project(key, base=None):
                        open_chunk(key)
                        open_group(key)
                        for k in range(KD):
                            if base is not None:
                                pe.wait_ge(xm_ready, KD * base + k + 1)
                            mm = mm3(gbank(key)[:, 0:TOK], weights(key, k * 128), xm_tile(k), k == 0, k == KD - 1)
                        mm.then_inc(chunk_used, 1)

                    def turn_values(n):
                        wait_freed(pe, V_KEYS[n])
                        open_group(("vt", n))
                        for c in range(NCH):
                            t = slice(c * 128, (c + 1) * 128)
                            mm = pe.transpose(gbank(("vt", n))[:, t], gu[:, n % 2, t], ident)
                        mm.then_inc(vt_done, 1)

                    def mod_chunk(q):
                        Q = q // 4
                        pe.wait_ge(mod_in[q % MODR], 16 * (q // MODR + 1))
                        if q % 4 == 0 and Q >= 2:
                            pe.wait_ge(mod_row, Q - 1)
                        for k in range(KD):
                            mm = pe.matmul(pb[1 + Q % 2][0:2, (q % 4) * 128:(q % 4 + 1) * 128], condT[:, k, :],
                                           modw[:, q % MODR, k * 128:(k + 1) * 128], start=k == 0, stop=k == KD - 1)
                        mm.then_inc(mod_done, 1)
                        if q % 4 == 3 and Q >= 1 and 4 * Q != mod_first:
                            mod_turn(Q - 1)

                    def mod_turn(Q):
                        pe.wait_ge(mod_row, Q + 1)
                        if 4 * Q == mod_first:
                            pe.wait_ge(mod_read, 1)
                        for i in range(4):
                            c = 2 * (4 * Q + i)
                            mm = pe.transpose(pb[0][:, c:c + 2], mrow[:, Q % 2, i * 128:(i + 1) * 128], ident[0:2, 0:2])
                        mm.then_inc(mod_t, 1)

                    def layer_norm(s, keyf):
                        for m in range(KD):
                            wait_freed(pe, keyf(m))
                            mm = pe.matmul(pb[1][:, 0:TOK], ones, x[:, m, :], start=m == 0, stop=m == KD - 1)
                        mm.then_inc(mean_done, 1)
                        for m in range(KD):
                            pe.wait_ge(sq_ready, KD * s + m + 1)
                            pe.matmul(pb[2][:, 0:TOK], ones, sq[:, m % 4, :], start=m == 0, stop=m == KD - 1
                                      ).then_inc(sq_used, 1)

                    def ffn(f):
                        done = mod_first
                        for i in range(2 * NF):
                            project(("ab"[i % 2], f, i // 2), 3 * f if i == 0 else None)
                            if f == 0:
                                for q in range(done, mod_after[i]):
                                    mod_chunk(q)
                                done = mod_after[i]
                        if f == 0:
                            mod_turn(NMODC // 4 - 1)
                        for m in range(KD):
                            open_group(("o", f, m))
                            for c in range(3):
                                key = ("o", f, m, c)
                                open_chunk(key)
                                for k in range(c * FH, min(NF, (c + 1) * FH)):
                                    if m == 0:
                                        pe.wait_ge(h_ready, NF * f + k + 1)
                                    mm = mm3(gbank(key[:3])[:, 0:TOK], weights(key, (k - c * FH) * 128),
                                             (h_hi[:, k, :], h_lo[:, k, :]), k == 0, k == NF - 1)
                                mm.then_inc(chunk_used, 1)
                        layer_norm(2 * f, lambda m: ("o", f, m))

                    def up(br, mp, hi, lo):
                        key = ("u", br, mp)
                        open_chunk(key)
                        for e in range(2):
                            gk = ("u", br, 2 * mp + e)
                            open_group(gk)
                            for k in range(NB):
                                mm = mm3(gbank(gk)[:, 0:TOK], weights(key, k * 256 + e * 128),
                                         (hi[:, k, :], lo[:, k, :]), k == 0, k == NB - 1)
                        mm.then_inc(chunk_used, 1)

                    pe.wait_ge(par_in, 16 * 14)
                    pe.transpose(pb[3][:, 0:120], pst[0:120, 0, :], ident[0:120, 0:120])
                    pe.transpose(pb[3][:, 120:174], pst[0:54, 1, :], ident[0:54, 0:54]).then_inc(par_t, 1)
                    for q in range(mod_first):
                        mod_chunk(q)
                    mod_turn(mod_first // 4 - 1)
                    ffn(0)

                    for i in range(C_BLOCKS):
                        project(("c", i), 1 if i == 0 else None)
                    for i in range(4):
                        project(("aq", i))
                    project(("ak", 0))
                    project(("av", 0))

                    pe.wait_ge(lam_in, 32)
                    pe.matmul(pb[3][:, 0:256], ones[0:1, :], t3[0:1, 0:256], start=True, stop=True).then_inc(lam_b, 1)
                    pe.wait_ge(cache_in, 64)
                    for i in range(5):
                        if i == 4:
                            pe.wait_ge(kc_ready, 1)
                        mm = pe.transpose(pb[0][:, (i % 4) * 128:(i % 4 + 1) * 128], kst[:, i, :], ident)
                        if i >= 3:
                            mm.then_inc(kt_done, 1)

                    turn_values(0)

                    def rotate(i, bank):
                        return pe.matmul(bank[:, 0:TS], cst[:, CO_ROT:CO_ROT + 128], qk[:, i, TP:TOK], start=True, stop=True)

                    pe.wait_ge(lam_dot, 1)
                    for i in range(6):
                        if i < 5:
                            project(B_QK[i])
                            pe.wait_ge(qsq_ready, i + 1)
                            pe.matmul(pb[1][:, 0:TOK], blk, t1[:, :], start=True, stop=True).then_inc(qms_done, 1)
                        if i >= 1:
                            pe.wait_ge(qn_ready, i)
                            if i >= 3:
                                pe.wait_ge(rope_ready, i - 2)
                            rotate(i - 1, pb[2 + (i - 1) % 2]).then_inc(rot_done, 1)
                    for key in B_QK[5:]:
                        project(key)
                    pe.wait_ge(rope_ready, 5)
                    pe.wait_ge(kc_ready, 2)
                    pe.matmul(pb[0][:, 0:TOK], cst[:, CO_SWAP:CO_SWAP + 128], qk[:, 4, :], start=True, stop=True)
                    pe.matmul(pb[0][:, TOK:TOK + PAST], cst[:, CO_SWAP:CO_SWAP + 128], kc[:, 0, :], start=True,
                              stop=True).then_inc(swap_done, 1)
                    for i in range(5):
                        if i == 1:
                            wait_freed(pe, ("bk", 3))
                        if i == 4:
                            pe.wait_ge(kout_ready, 1)
                        mm = pe.transpose(pb[1][:, (i % 4) * 128:(i % 4 + 1) * 128], qk[:, (4, 9, 10, 11, 12)[i], 0:TP], ident)
                        if i >= 3:
                            mm.then_inc(kout_t, 1)
                    pe.wait_ge(swap_ready, 1)
                    pe.wait_ge(kout_ready, 2)
                    wait_freed(pe, ("vt", 0))

                    def scores(un):
                        tile, c = un["tile"], un["c"]
                        if tile == NB and c == 0:
                            pe.wait_ge(rope_ready, 13)
                        for n, e in un["sets"]:
                            if n >= 2:
                                pe.wait_ge(exp_done, n - 1)
                            p = slice(HD * e, HD * e + HD)
                            if tile >= NB:
                                q, kn, kp = qk[p, 5 + tile - NB, :], qk[p, 9 + tile - NB, :], kc[p, 1 + tile - NB, :]
                            elif (2 * tile + e) // 4 == e:
                                q, kn, kp = qk[p, tile, :], qk[p, 4, :], kc[p, 0, :]
                            else:
                                q, kn, kp = qk[p, tile, :], kswap[p, 0:TOK], kswap[p, TOK:TOK + PAST]
                            q = q[:, c * 128:(c + 1) * 128]
                            if c == 0:
                                mm = pe.matmul(pb[n % 2][:, 0:TP], q, kn[:, 0:TP], start=True, stop=True)
                            else:
                                pe.matmul(pb[n % 2][:, 0:TS], q, kn[:, TP:TOK], start=True, stop=True)
                                mm = pe.matmul(pb[n % 2][:, TS:TOK], q, kp, start=True, stop=True)
                            mm.then_inc(scored, 1)

                    def turn(un):
                        u, slot = un["u"], un["sets"][-1][0] % 4
                        pe.wait_ge(probs_ready, u + 1)
                        if u >= 1:
                            pe.wait_ge(probs_t_ready, u)
                        for k in range(1 if un["c"] == 0 else 3):
                            mm = pe.transpose(pb[2][:, k * 128:(k + 1) * 128], pr[:, slot, k * 128:(k + 1) * 128], ident)
                        mm.then_inc(probs_t, 1)

                    def weigh(un):
                        u, c, tile, e = un["u"], un["c"], un["tile"], un["e"]
                        nk = 1 if c == 0 else 3
                        pe.wait_ge(probs_t_ready, u + 1)
                        if tile == NB and un["first"]:
                            wait_freed(pe, ("vt", NB))
                        if un["first"] and tile > NB:
                            pe.wait_ge(sub_std, tile - NB)
                        elif un["first"] and tile >= 1:
                            pe.wait_ge(branch_ready, tile)
                        for k in range(nk):
                            tok = 0 if c == 0 else k + 1
                            if tile < NB:
                                kv = (2 * tile + e) // 4
                                vals = va[:, tok, HD * kv:HD * kv + HD]
                                out = pb[3][HD * e:HD * e + HD, c * 128:(c + 1) * 128]
                            else:
                                vals = vb[:, tok, (tile - NB) * 128:(tile - NB + 1) * 128]
                                out = pb[3][:, c * 128:(c + 1) * 128]
                            mm = pe.matmul(out, vals, pT[:, u % 2, k, :], start=k == 0, stop=k == nk - 1)
                        mm.then_inc(weighted_done, 1)

                    def sub_sums(un):
                        pe.wait_ge(sub_sq, un["tile"] - NB + 1)
                        pe.matmul(pb[3][:, 0:TOK], ones, t1[:, :], start=True, stop=True).then_inc(sub_ms, 1)

                    def filler(key):
                        if key[0] == "rot":
                            open_group(key)
                            rotate(key[1], gbank(key)).then_inc(rot_done, 1)
                        elif key[0] == "vt":
                            turn_values(key[1])
                        elif key[0] == "u":
                            if key[2] == 0:
                                pe.wait_ge(branch_ready, NB)
                            up(*key[1:], br_hi, br_lo)
                        else:
                            project(key)

                    for u, un in enumerate(units):
                        if u >= 1:
                            turn(units[u - 1])
                        scores(un)
                        if u >= 2 and units[u - 2]["last"] and units[u - 2]["tile"] >= NB:
                            sub_sums(units[u - 2])
                        for key in fillers[u]:
                            filler(key)
                        if u >= 1:
                            weigh(units[u - 1])
                    turn(units[-1])
                    weigh(units[-1])
                    sub_sums(units[-1])
                    pe.wait_ge(branch_ready, 2 * NB)
                    for mp in range(KD // 2):
                        up(1, mp, br_hi, br_lo)

                    pe.wait_ge(cmix_ready, C_BLOCKS)
                    for c in range(NCH):
                        for j in range(NB):
                            mm = pe.transpose(pb[c][:, j * 128:(j + 1) * 128], cmix[:, 8 + j, c * 128:(c + 1) * 128], ident)
                        mm.then_inc(vtok_t, 1)
                    pe.wait_ge(vtok_ready, NCH)
                    pe.wait_ge(lora_in, 48)
                    pe.wait_ge(lora_act, 2)
                    for m in range(KD - ACC, KD):
                        wait_freed(pe, ("u", 1, m))

                    def prepare_decay(g):
                        j, d = g // 2, g % 2
                        if g % 2 == 0:
                            pe.wait_ge(kk_std, g // 2 + 1)
                        else:
                            pe.wait_ge(gram_read, 6 * g)
                            pe.wait_ge(lt_ready, 6 * g)
                        pe.matmul(acc[1][:, 0:TOK], lora_w[64 * d:64 * d + 64, j * 128:(j + 1) * 128],
                                  cmix[64 * d:64 * d + 64, 12, :], start=True, stop=True).then_inc(lora_decay, 1)

                    def prepare_rate(g):
                        j, d = g // 2, g % 2
                        pe.wait_ge(decay_done, g + 1)
                        pe.matmul(acc[1][:, 0:TOK], lora_a[64 * d:64 * d + 64, j * 128:(j + 1) * 128],
                                  cmix[64 * d:64 * d + 64, 13, :], start=True, stop=True).then_inc(lora_done, 1)

                    def prepare_norm(g):
                        pe.wait_ge(kk_sq, g // 2 + 1)
                        if g >= 1:
                            pe.wait_ge(gram_read, 6 * g)
                            pe.wait_ge(lt_ready, 6 * g)
                        pe.matmul(acc[1][:, 0:TOK], blk, bt[:, :], start=True, stop=True).then_inc(kk_ms, 1)

                    def prepare_tok(g):
                        if g >= 2:
                            pe.wait_ge(sa_ready, 3 * (g - 1))
                        pe.wait_ge(ab_ready, g + 1)
                        for c in range(NCH):
                            t = slice(c * 128, (c + 1) * 128)
                            pe.transpose(acc[0][:, t], bt[:, t], ident)
                            mm = pe.transpose(acc[1][:, t], kt[:, t], ident)
                        mm.then_inc(tok_t, 1)

                    def prepare_gram(g, f):
                        n = 6 * g + f
                        if f < 2:
                            pe.wait_ge(tok_ready, g + 1)
                        else:
                            pe.wait_ge(gram_read, n - 1)
                            pe.wait_ge(lt_ready, n - 1)
                        c, hh = f // 2, f % 2
                        hp = slice(64 * hh, 64 * hh + 64)
                        for i in range(2):
                            lhs = (bt, kt)[i][hp, c * 128:(c + 1) * 128]
                            mm = pe.matmul(acc[n % 2][:, i * 256:(i + 1) * 256], lhs,
                                           ar[hp, g % 2, c, :, :].rearrange("p a t -> p (a t)"), start=True, stop=True)
                        mm.then_inc(gram_done, 1)

                    def turn_start(g):
                        pe.wait_ge(xt0_ready, g + 1)
                        for h in range(2):
                            if g >= 1:
                                pe.wait_ge(xi_ready, 2 * NL * g - 1 + h)
                            for u in range(3):
                                mm = pe.transpose(pb[h][:, u * 128:(u + 1) * 128], xt[:, g % 2, 3 * h + u, :], ident)
                            mm.then_inc(xi_t, 1)

                    def level_lx(g, n):
                        pe.wait_ge(ltm_ready, NL * g + n)
                        for h in range(2):
                            at = 2 * (NL * g + n - 1) + h + 1
                            if n == 1:
                                pe.wait_ge(xi0_ready, 2 * g + h + 1)
                            else:
                                pe.wait_ge(xi_ready, at - 2)
                            for u in range(3):
                                mm = pe.matmul(pb[h][:, u * 128:(u + 1) * 128], ltm[:, 3 * h + u, :], xi[:, 3 * h + u, :],
                                               start=True, stop=True)
                            mm.then_inc(tl_done, 1)

                    def level_xlx(g, n):
                        for h in range(2):
                            at = 2 * (NL * g + n - 1) + h + 1
                            pe.wait_ge(tl_ready, at)
                            if at > 2:
                                pe.wait_ge(xt_ready, at - 2)
                            for u in range(3):
                                mm = pe.matmul(pb[h][:, u * 128:(u + 1) * 128], xt[:, g % 2, 3 * h + u, :],
                                               tl[:, 3 * h + u, :], start=True, stop=True)
                            mm.then_inc(u_done, 1)

                    def level_turn(g, n):
                        for h in range(2):
                            pe.wait_ge(xi_ready, 2 * (NL * g + n - 1) + h + 1)
                            for u in range(3):
                                mm = pe.transpose(pb[2 + h][:, u * 128:(u + 1) * 128], xi[:, 3 * h + u, :], ident)
                            mm.then_inc(xt_t, 1)

                    def heads(g, c):
                        j = g // 2
                        return [(slice(64 * hh, 64 * hh + 64), 3 * hh + c, vtok[:, c, j * 128 + 64 * hh:j * 128 + 64 * hh + 64])
                                for hh in range(2)]

                    def scan_right(g, i):
                        c = scan_order(g)[i]
                        if i == 0:
                            if g < 2 * NB - 1:
                                pe.wait_ge(tok_ready, g + 2)
                                pe.wait_ge(gram_read, 6 * g + 12)
                                pe.wait_ge(lt_ready, 6 * g + 12)
                            pe.wait_ge(state_in, 32 * (g + 1))
                            pe.transpose(acc[1][:, 0:128], sld[:, :], ident).then_inc(state_t, 1)
                        if i >= 1:
                            pe.wait_ge(sp_ready, 2 * g + i)
                        for hs, u, v in heads(g, c):
                            if i >= 1:
                                pe.matmul(acc[0][:, hs], ar[:, g % 2, c, 0, :], sp[:, hs], start=True, stop=False)
                            mm = pe.matmul(acc[0][:, hs], lak[:, g % 2, u, :], v, start=i == 0, stop=True)
                        mm.then_inc(r_done, 1)

                    def scan_solve(g, i):
                        c, n = scan_order(g)[i], 3 * g + i
                        if i == 0:
                            pe.wait_ge(xt_ready, 2 * NL * (g + 1))
                        pe.wait_ge(r_ready, n + 1)
                        for hs, u, _ in heads(g, c):
                            mm = pe.matmul(acc[0][:, 128 + hs.start:128 + hs.stop], xt[:, g % 2, u, :], rs[:, hs],
                                           start=True, stop=True)
                        mm.then_inc(sa_done, 1)

                    def scan_out(g, i):
                        c, n = scan_order(g)[i], 3 * g + i
                        pe.wait_ge(sa_ready, n + 1)
                        if n >= 1:
                            pe.wait_ge(o_read, n)
                        if i == 0 and g >= 1:
                            pe.wait_ge(sp_ready, 2 * g)
                            pe.wait_ge(spo_ready, g)
                            if g % 2 == 0:
                                pe.wait_ge(out_done, g // 2)
                        if i >= 1:
                            pe.matmul(acc[2][:, 0:128], sp[:, :], ar[:, g % 2, c, 1, :], start=True, stop=False)
                        for hs, u, v in heads(g, c):
                            pe.matmul(acc[2][hs, 0:128], sas[:, hs], rbk[:, g % 2, u, 0, :], start=i == 0, stop=False)
                            mm = pe.matmul(acc[2][hs, 0:128], v, rbk[:, g % 2, u, 1, :], start=False, stop=True)
                        mm.then_inc(o_done, 1)
                        if i < 2:
                            pe.wait_ge(sp_ready, 2 * g + 1)
                            if i == 1:
                                pe.wait_ge(spo_ready, g + 1)
                            for hs, u, v in heads(g, c):
                                pe.matmul(acc[3][hs, hs], btok[:, g % 2, c, hs], sas[:, hs], start=True, stop=False)
                                mm = pe.matmul(acc[3][hs, hs], ktok[:, g % 2, c, hs], v, start=False, stop=True)
                            mm.then_inc(sn_done, 1)

                    def scan_turn(g):
                        pe.wait_ge(sn_read, g + 1)
                        pe.transpose(acc[3][:, 128:256], spo[:, :], ident).then_inc(spo_t, 1)

                    def tile_sums(j):
                        pe.wait_ge(o_read, 3 * (2 * j + 2))
                        pe.matmul(acc[2][:, 0:TOK], blk, osum[:, :], start=True, stop=True).then_inc(gn_mean, 1)
                        pe.wait_ge(bonus_in, j + 1)
                        pe.wait_ge(sp_ready, 2 * (2 * j + 2))
                        pe.matmul(acc[3][:, 0:TOK], blk, guc[:, 0, :], start=True, stop=True).then_inc(bonus_sum, 1)

                    def tile_var(j):
                        pe.wait_ge(gn_sq, j + 1)
                        pe.matmul(acc[2][:, 0:TOK], blk, guc[:, 1, :], start=True, stop=True).then_inc(gn_var, 1)

                    def tile_gate(j):
                        pe.wait_ge(bonus_read, j + 1)
                        pe.matmul(acc[3][:, 0:TOK], lora_g[:, j * 128:(j + 1) * 128], cmix[:, 14, :], start=True, stop=True
                                  ).then_inc(out_gate, 1)

                    prepare_norm(0)
                    prepare_decay(0)
                    prepare_rate(0)
                    prepare_tok(0)
                    for f in range(6):
                        prepare_gram(0, f)
                    turn_start(0)
                    for g in range(2 * NB + 1):
                        inv, scan, nxt = g < 2 * NB, g >= 1, g + 1 < 2 * NB
                        tail = scan and g % 2 == 0
                        for n in range(1, NL + 1):
                            if inv:
                                level_lx(g, n)
                            if scan and n <= 3:
                                scan_right(g - 1, n - 1)
                            if tail and n == 4:
                                tile_sums(g // 2 - 1)
                            if nxt and n == 5:
                                prepare_gram(g + 1, 0)
                                prepare_gram(g + 1, 1)
                            if inv:
                                level_xlx(g, n)
                            if scan and n <= 3:
                                scan_solve(g - 1, n - 1)
                            if tail and n == 4:
                                tile_var(g // 2 - 1)
                            if nxt and n == 5:
                                prepare_gram(g + 1, 2)
                                prepare_gram(g + 1, 3)
                            if inv:
                                level_turn(g, n)
                            if scan and n <= 3:
                                scan_out(g - 1, n - 1)
                                if n == 1:
                                    scan_turn(g - 1)
                            if nxt and n == 1:
                                if g % 2 == 1:
                                    prepare_norm(g + 1)
                                prepare_decay(g + 1)
                            if nxt and n == 2:
                                prepare_rate(g + 1)
                            if tail and n == 4:
                                tile_gate(g // 2 - 1)
                            if nxt and n == 4:
                                prepare_tok(g + 1)
                            if nxt and n == 5:
                                prepare_gram(g + 1, 4)
                                prepare_gram(g + 1, 5)
                        if nxt:
                            turn_start(g + 1)
                    pe.wait_ge(brc_ready, NB)
                    for mp in range(KD // 2):
                        up(2, mp, brc_hi, brc_lo)

                    for m in range(KD):
                        project(("w", m), 2 if m == 0 else None)
                    layer_norm(1, lambda m: ("w", m))
                    ffn(1)

                @block.scalar
                def _(act):
                    link, done, freed = linker(act, ach)
                    nsplit = [0]

                    def splits_to(n):
                        for c in range(nsplit[0], min(n + 1, NCHUNK)):
                            act.wait_ge(raw_in[c % RAW], 16 * (c // RAW + 1))
                            if c >= SPL:
                                act.wait_ge(chunk_used, c - SPL + 1)
                            w = chunk_len(chunk_list[c])
                            done(act.activation(w_hi[:, c % SPL, 0:w], raw[:, c % RAW, 0:w], ACT.Copy), hi_done)
                            nsplit[0] = c + 1

                    def ahead(key):
                        splits_to(chunk_no[key] + LOOK)

                    def xm_high(s, base):
                        for m in range(KD):
                            act.wait_ge(xf_ready, KD * s + m + 1)
                            done(act.activation(xm_hi[:, m, :], sq[:, m % 4, :], ACT.Copy), xhi_ready)

                    def h_high(f, j):
                        wait_freed(act, ("b", f, j))
                        done(act.activation(h_hi[:, j, :], hf[:, j % 2, :], ACT.Copy), hhi_done)

                    def ffn(f):
                        for j in range(NF):
                            ka, kb = ("a", f, j), ("b", f, j)
                            ahead(ka)
                            wait_group(act, ka)
                            if j >= 2:
                                wait_freed(act, ("b", f, j - 2))
                            freed(act.activation(sa[:, j % 2, :], gbank(ka)[:, 0:TOK], ACT.Silu), ka)
                            ahead(kb)
                            if j >= 1:
                                h_high(f, j - 1)
                        h_high(f, NF - 1)
                        for m in range(KD):
                            for c in range(3):
                                ahead(("o", f, m, c))

                    def layer_norm(s):
                        for m in range(KD):
                            act.wait_ge(d_ready, KD * s + m + 1)
                            if m >= 4:
                                act.wait_ge(sq_used, KD * s + m - 3)
                            done(act.activation(sq[:, m % 4, :], x[:, m, :], ACT.Square), sq_ready)
                        act.wait_ge(sq_used, KD * (s + 1))
                        done(act.activation(mean[:, :], pb[2][:, 0:TOK], ACT.Sqrt, scale=1.0 / D, bias=eps[:, 0:1]), std_done)
                        for m in range(KD):
                            act.wait_ge(n_ready, KD * s + m + 1)
                            done(act.activation(x[:, m, :], x[:, m, :], ACT.Identity, scale=par[:, 72 + KD * s + m:73 + KD * s + m],
                                           bias=par[:, 96 + KD * s + m:97 + KD * s + m]), x_ready)

                    splits_to(LOOK - 1)
                    xm_high(0, 0)
                    ffn(0)
                    layer_norm(0)
                    xm_high(1, 1)

                    act.wait_ge(pads, 1)
                    for i in range(C_BLOCKS):
                        key = ("c", i)
                        ahead(key)
                        wait_group(act, key)
                        if i >= 3:
                            act.wait_ge(cmix_ready, i - 2)
                        link(act.activation(cin[:, i % 3, 1:1 + TP], gbank(key)[:, 0:TP], ACT.Copy))
                        freed(act.activation(cin[:, i % 3, 3 + TP:3 + TOK], gbank(key)[:, TP:TOK], ACT.Copy), key)
                    def take(key):
                        wait_group(act, key)
                        bank = gbank(key)[:, 0:TOK]
                        if key[0] == "g":
                            if key[1] == 2:
                                act.wait_ge(kv_out, 64)
                            gate = (merged, gate1, gate2)[key[1]]
                            freed(act.activation(gate[:, key[2], :], bank, ACT.Tanh, scale=0.5), key)
                        else:
                            freed(act.activation(qk[:, qk_keys.index(key), :], bank, ACT.Copy), key)

                    for key in qk_keys[0:5]:
                        ahead(key)
                        take(key)
                    ahead(("av", 0))
                    act.wait_ge(lam_dot, 1)
                    done(act.activation(lam[:, 2:4], lam[:, 0:2], ACT.Exp), lam_exp)
                    for i in range(5):
                        if i >= 1:
                            act.wait_ge(qms_done, i)
                        else:
                            act.wait_ge(lam_b, 1)
                        done(act.activation(t1[:, :], qk[:, i, :], ACT.Square), qsq_ready)
                        ahead(B_QK[i])
                        take(B_QK[i])
                        act.wait_ge(qms_done, i + 1)
                        if i >= 1:
                            act.wait_ge(qn_ready, i)
                        done(act.activation(t2[:, :], pb[1][:, 0:TOK], ACT.Sqrt, scale=1.0 / HD, bias=eps[:, 1:2]), qstd_done)
                    for key in B_QK[5:]:
                        ahead(key)
                        take(key)
                    act.wait_ge(cmix_ready, C_BLOCKS)

                    def copy_turned(un):
                        u, w = un["u"], 128 if un["c"] == 0 else TOK
                        act.wait_ge(probs_t, u + 1)
                        if u >= 2:
                            act.wait_ge(weighted_done, u - 1)
                        done(act.activation(pT[:, u % 2, :, :].rearrange("p k t -> p (k t)")[:, 0:w], pb[2][:, 0:w], ACT.Copy
                                       ), probs_t_ready)

                    def exps(un):
                        w = 128 if un["c"] == 0 else TOK
                        for n, _ in un["sets"]:
                            act.wait_ge(max_done, n + 1)
                            if n >= 4:
                                act.wait_ge(probs_t, set_unit[n - 4] + 1)
                            done(act.activation(pr[:, n % 4, 0:w], pb[n % 2][:, 0:w], ACT.Exp, scale=SCALE,
                                           bias=st[:, n % 4, 1:2], accum_out=st[:, n % 4, 2:3]), exp_done)

                    def finish_a(un):
                        act.wait_ge(weighted_done, un["u"] + 1)
                        done(act.activation(br_hi[:, un["tile"], :], pb[3][:, 0:TOK], ACT.Copy), branch_hi)

                    def sub_square(un):
                        act.wait_ge(tile_read, un["tile"] - NB + 1)
                        done(act.activation(t1[:, :], t2[:, :], ACT.Square), sub_sq)

                    def sub_root(un):
                        act.wait_ge(sub_ms, un["tile"] - NB + 1)
                        done(act.activation(t3[:, :], pb[3][:, 0:TOK], ACT.Sqrt, scale=1.0 / 128, bias=eps[:, 1:2]), sub_std)

                    def sub_high(un):
                        k = un["tile"] - NB
                        if k == 0:
                            act.wait_ge(chunk_used, chunk_no[("u", 0, KD // 2 - 1)] + 1)
                        act.wait_ge(sub_done, k + 1)
                        done(act.activation(br_hi[:, k, :], t2[:, :], ACT.Copy), branch_hi)

                    for u, un in enumerate(units):
                        if u >= 1:
                            copy_turned(units[u - 1])
                        exps(un)
                        sub = u >= 2 and units[u - 2]["last"] and units[u - 2]["tile"] >= NB
                        if sub:
                            sub_root(units[u - 2])
                        for key in fillers[u]:
                            if key[0] not in ("rot", "vt"):
                                ahead(key)
                        for key in fillers[u]:
                            if key[0] == "g":
                                take(key)
                        if sub:
                            sub_high(units[u - 2])
                        if u >= 1 and units[u - 1]["last"]:
                            (finish_a if un["tile"] <= NB and units[u - 1]["tile"] < NB else sub_square)(units[u - 1])
                    copy_turned(units[-1])
                    sub_square(units[-1])
                    sub_root(units[-1])
                    sub_high(units[-1])
                    for mp in range(KD // 2):
                        ahead(("u", 1, mp))

                    act.wait_ge(cmix_ready, C_BLOCKS)
                    done(act.activation(cmix[:, 12, :], cmix[:, 12, :], ACT.Tanh), lora_act)
                    done(act.activation(cmix[:, 14, :], cmix[:, 14, :], ACT.Sigmoid), lora_act)

                    def prepare_decay(g):
                        j, d = g // 2, g % 2
                        act.wait_ge(lora_decay, g + 1)
                        done(act.activation(sg[:, :], acc[1][:, 0:TOK], ACT.Sigmoid, bias=par[:, 135 + 4 * d + j:136 + 4 * d + j]
                                       ), decay_done)

                    def prepare_rate(g):
                        j, d = g // 2, g % 2
                        act.wait_ge(lora_done, g + 1)
                        done(act.activation(aa[:, :], acc[1][:, 0:TOK], ACT.Sigmoid, bias=par[:, 143 + 4 * d + j:144 + 4 * d + j]
                                       ), sg_done)

                    def prepare_square(j):
                        act.wait_ge(kk_raw, j + 1)
                        done(act.activation(bt[:, :], kk[:, :], ACT.Square), kk_sq)

                    def prepare_norm(j):
                        act.wait_ge(kk_ms, j + 1)
                        done(act.activation(bt[:, :], acc[1][:, 0:TOK], ACT.Sqrt, bias=eps[:, 3:4]), kk_std)

                    def prepare_exps(g):
                        act.wait_ge(z_ready, g + 1)
                        link(act.activation(sg[:, :], zi[:, :], ACT.Exp, scale=-KAPPA))
                        link(act.activation(zx[:, :], zx[:, :], ACT.Exp, scale=-KAPPA))
                        link(act.activation(zi[:, :], zi[:, :], ACT.Exp, scale=KAPPA))
                        done(act.activation(eh[:, g % 2, :], half[:, :], ACT.Exp, scale=-KAPPA), exps_done)

                    def prepare_tok(g):
                        act.wait_ge(tok_t, g + 1)
                        link(act.activation(btok[:, g % 2, :, :].rearrange("p c k -> p (c k)"), acc[0][:, 0:TOK], ACT.Copy))
                        done(act.activation(ktok[:, g % 2, :, :].rearrange("p c k -> p (c k)"), acc[1][:, 0:TOK], ACT.Copy
                                       ), tok_ready)

                    def prepare_gram(g, f):
                        n = 6 * g + f
                        if g >= 2:
                            act.wait_ge(ltm_ready, NL * (g - 1))
                        act.wait_ge(gram_done, n + 1)
                        done(act.activation(lt[g % 2][:, 3 * (f % 2) + f // 2, :], acc[n % 2][:, 0:128], ACT.Copy), lt_ready)

                    def copy_start(g):
                        for h in range(2):
                            act.wait_ge(xi_t, 2 * g + h + 1)
                            if g >= 1:
                                act.wait_ge(xt_t, 2 * NL * g)
                            done(act.activation(xi[:, 3 * h:3 * h + 3, :].rearrange("p u s -> p (u s)"), pb[h][:, 0:TOK], ACT.Copy
                                           ), xi0_ready)

                    def level_lx(g, n):
                        for h in range(2):
                            act.wait_ge(tl_done, 2 * (NL * g + n - 1) + h + 1)
                            done(act.activation(tl[:, 3 * h:3 * h + 3, :].rearrange("p u s -> p (u s)"), pb[h][:, 0:TOK], ACT.Copy
                                           ), tl_ready)

                    def level_turn(g, n):
                        for h in range(2):
                            act.wait_ge(xt_t, 2 * (NL * g + n - 1) + h + 1)
                            done(act.activation(xt[:, g % 2, 3 * h:3 * h + 3, :].rearrange("p u s -> p (u s)"), pb[2 + h][:, 0:TOK],
                                                ACT.Copy), xt_ready)

                    def scan_right(g, i):
                        act.wait_ge(r_done, 3 * g + i + 1)
                        done(act.activation(rs[:, :], acc[0][:, 0:128], ACT.Copy), r_ready)

                    def scan_turn(g):
                        act.wait_ge(spo_t, g + 1)
                        if g >= 1:
                            act.wait_ge(st_out, 32 * g)
                        done(act.activation(spt[:, :], acc[3][:, 128:256], ACT.Copy), spo_ready)

                    def tile_square(j):
                        act.wait_ge(gn_centred, j + 1)
                        done(act.activation(guc[:, 1, :], osum[:, :], ACT.Square), gn_sq)

                    def tile_std(j):
                        act.wait_ge(gn_var, j + 1)
                        done(act.activation(guc[:, 1, :], acc[2][:, 0:TOK], ACT.Sqrt, scale=1.0 / HD, bias=eps[:, 2:3]), gn_std)

                    def tile_high(j):
                        act.wait_ge(out_done, j + 1)
                        done(act.activation(brc_hi[:, j, :], osum[:, :], ACT.Copy), brc_hi_s)

                    prepare_square(0)
                    prepare_norm(0)
                    prepare_decay(0)
                    prepare_rate(0)
                    prepare_exps(0)
                    prepare_tok(0)
                    for f in range(6):
                        prepare_gram(0, f)
                    copy_start(0)
                    for g in range(2 * NB + 1):
                        inv, scan, nxt = g < 2 * NB, g >= 1, g + 1 < 2 * NB
                        tail = scan and g % 2 == 0
                        for n in range(1, NL + 1):
                            if inv:
                                level_lx(g, n)
                            if g >= 3 and g % 2 == 1 and n == 1:
                                tile_high(g // 2 - 1)
                            if scan and n <= 3:
                                scan_right(g - 1, n - 1)
                            if nxt and n == 1 and g % 2 == 1:
                                prepare_square((g + 1) // 2)
                            if tail and n == 4:
                                tile_square(g // 2 - 1)
                            if nxt and n == 5:
                                prepare_gram(g + 1, 0)
                                prepare_gram(g + 1, 1)
                                prepare_gram(g + 1, 2)
                                prepare_gram(g + 1, 3)
                            if inv:
                                level_turn(g, n)
                            if scan and n == 1:
                                scan_turn(g - 1)
                            if nxt and n == 1:
                                if g % 2 == 1:
                                    prepare_norm((g + 1) // 2)
                                prepare_decay(g + 1)
                            if nxt and n == 2:
                                prepare_rate(g + 1)
                            if nxt and n == 3:
                                prepare_exps(g + 1)
                            if tail and n == 4:
                                tile_std(g // 2 - 1)
                            if nxt and n == 4:
                                prepare_tok(g + 1)
                            if nxt and n == 5:
                                prepare_gram(g + 1, 4)
                                prepare_gram(g + 1, 5)
                        if nxt:
                            copy_start(g + 1)
                    tile_high(NB - 1)
                    for mp in range(KD // 2):
                        ahead(("u", 2, mp))
                    act.wait_ge(merged_done, 2 * KD)
                    for m in range(KD):
                        done(act.activation(xm_hi[:, m, :], merged[:, m, :], ACT.Copy, scale=0.5), xhi_ready)
                    for m in range(KD):
                        ahead(("w", m))
                    layer_norm(1)
                    xm_high(2, 3)
                    ffn(1)
                    layer_norm(2)

                @block.gpsimd
                def _(pool):
                    link, done, freed = linker(pool, pch)

                    def scale_x(s, n):
                        pool.wait_ge(xm_ready, n)
                        xf = x[:, :, :].rearrange("p k t -> p (k t)")
                        done(pool.tensor_scalar(xf, xf, ALPHA, 1.0, ALU.mult, ALU.mult), scaled)

                    scale_x(0, KD)
                    pool.wait_ge(xm_ready, 2 * KD)
                    done(pool.memset(cin[:, :, :], 0.0), pads)
                    scale_x(1, 2 * KD)
                    for i in range(C_BLOCKS):
                        wait_freed(pool, ("c", i))
                        if i >= 2:
                            pool.wait_ge(cmix_ready, i - 1)
                        done(pool.tensor_tensor(csum[:, i % 2, :], cin[:, i % 3, 0:386], cin[:, i % 3, 2:388], ALU.add
                                           ), csum_ready)
                    pool.wait_ge(merged_done, KD)
                    pool.wait_ge(kv_out, 64)
                    link(pool.memset(sld[:, :], 0.0))
                    done(pool.memset(spo[:, :], 0.0), pads)
                    for g in range(2 * NB):
                        d = g % 2
                        for n in range(1, len(LEVELS)):
                            if n == 1:
                                pool.wait_ge(lt_ready, 6 * g + 6)
                            if g >= 1 or n >= 2:
                                pool.wait_ge(tl_done, 2 * (NL * g + n - 1))
                            o = CO_LEV + (d * len(LEVELS) + n) * 128
                            done(pool.tensor_tensor(ltm[:, :, :], lt[g % 2][:, :, :], over(cst[:, o:o + 128], 6), ALU.mult
                                               ), ltm_ready)
                    scale_x(2, 4 * KD)

                @block.vector
                def _(dve):
                    link, done, freed = linker(dve, dch)
                    nsplit = [0]

                    def splits_to(n):
                        for c in range(nsplit[0], min(n + 1, NCHUNK)):
                            dve.wait_ge(hi_done, c + 1)
                            w = chunk_len(chunk_list[c])
                            done(dve.tensor_tensor(w_lo[:, c % SPL, 0:w], raw[:, c % RAW, 0:w],
                                              w_hi[:, c % SPL, 0:w].bitcast(F32), ALU.subtract), lo_done)
                            nsplit[0] = c + 1

                    def ahead(key):
                        splits_to(chunk_no[key] + LOOK)

                    def modulate(s, base):
                        def low(m):
                            dve.wait_ge(xhi_ready, KD * base + m + 1)
                            done(dve.tensor_tensor(xm_lo[:, m, :], sq[:, m % 4, :], xm_hi[:, m, :].bitcast(F32), ALU.subtract
                                              ), xm_ready)
                        for m in range(KD):
                            if s > 0:
                                dve.wait_ge(x_ready, KD * (s - 1) + m + 1)
                            for gi, (a, b) in enumerate(GROUPS):
                                ins = dve.tensor_scalar(sq[:, m % 4, a:b], x[:, m, a:b], modv[:, 3 * s + 1, m, gi:gi + 1],
                                                        modv[:, 3 * s, m, gi:gi + 1], ALU.mult, ALU.add)
                            done(ins, xf_ready)
                            if m >= 1:
                                low(m - 1)
                        low(KD - 1)

                    def residual(s, key, m):
                        wait_group(dve, key)
                        dve.wait_ge(scaled, s + 1)
                        for gi, (a, b) in enumerate(GROUPS):
                            ins = dve.scalar_tensor_tensor(out=x[:, m, a:b], in0=gbank(key)[:, a:b],
                                                           scalar=modv[:, 3 * s + 2, m, gi:gi + 1], in1=x[:, m, a:b],
                                                           op0=ALU.mult, op1=ALU.add)
                        freed(ins, key)

                    def layer_norm(s):
                        dve.wait_ge(mean_done, s + 1)
                        for m in range(KD):
                            done(dve.scalar_tensor_tensor(out=x[:, m, :], in0=pb[1][:, 0:TOK], scalar=-1.0 / D, in1=x[:, m, :],
                                                     op0=ALU.mult, op1=ALU.add), d_ready)
                        dve.wait_ge(std_done, s + 1)
                        link(dve.reciprocal(rstd[:, :], mean[:, :]))
                        for m in range(KD):
                            done(dve.tensor_tensor(x[:, m, :], x[:, m, :], rstd[:, :], ALU.mult), n_ready)

                    def h_low(f, j):
                        dve.wait_ge(hhi_done, NF * f + j + 1)
                        done(dve.tensor_tensor(h_lo[:, j, :], hf[:, j % 2, :], h_hi[:, j, :].bitcast(F32), ALU.subtract
                                          ), h_ready)

                    def ffn(f):
                        for j in range(NF):
                            ka, kb = ("a", f, j), ("b", f, j)
                            ahead(ka)
                            ahead(kb)
                            wait_freed(dve, ka)
                            wait_group(dve, kb)
                            freed(dve.tensor_tensor(hf[:, j % 2, :], sa[:, j % 2, :], gbank(kb)[:, 0:TOK], ALU.mult
                                              ), kb)
                            if j >= 1:
                                h_low(f, j - 1)
                            if f == 0:
                                copy_rows(mod_after[2 * j] // 4)
                        if f == 0:
                            copy_rows(NMODC // 4)
                        h_low(f, NF - 1)
                        if f == 0:
                            dve.wait_ge(mod_t, NMODC // 4)
                            take_mod(2, N_MOD)
                        for m in range(KD):
                            for c in range(3):
                                ahead(("o", f, m, c))
                            residual(2 * f, ("o", f, m), m)
                        layer_norm(2 * f)

                    rows_copied = [0]

                    def copy_rows(n):
                        for Q in range(rows_copied[0], n):
                            dve.wait_ge(mod_done, 4 * Q + 4)
                            if Q >= 2:
                                dve.wait_ge(mod_t, Q - 1)
                            done(dve.tensor_copy(mrow[:, Q % 2, :], pb[1 + Q % 2][0:2, :]), mod_row)
                            rows_copied[0] = Q + 1

                    def take_mod(a, b):
                        n0, n1 = a * KD, b * KD
                        mv = modv[:, :, :, :].rearrange("p n k g -> p (n k) g")
                        for gi in range(2):
                            ins = dve.tensor_tensor(mv[:, n0:n1, gi], pb[0][:, 0:2 * NMODC].rearrange("p (n g) -> p n g", g=2)[:, n0:n1, gi],
                                                    par[:, n0:n1], ALU.add)
                            link(ins)
                        for i in range(a, b):
                            if i % 3 == 1:
                                link(dve.tensor_scalar(modv[:, i, :, :], modv[:, i, :, :], 1.0, None, ALU.add))
                            elif i in (2, 8):
                                link(dve.tensor_scalar(modv[:, i, :, :], modv[:, i, :, :], 0.5, None, ALU.mult))

                    dve.wait_ge(par_t, 1)
                    link(dve.tensor_copy(par[:, 0:174], pb[3][:, 0:174]))
                    link(dve.tensor_scalar(small[:, 8:12], par[:, 155:159], -1.0, 1.0, ALU.mult, ALU.add))
                    copy_rows(mod_first // 4)
                    dve.wait_ge(mod_t, mod_first // 4)
                    take_mod(0, 2)
                    dve.nop().then_inc(mod_read, 1)
                    splits_to(LOOK - 1)
                    modulate(0, 0)
                    ffn(0)
                    modulate(1, 1)

                    for i in range(C_BLOCKS):
                        ahead(("c", i))
                        dve.wait_ge(csum_ready, i + 1)
                        mu = par[:, 120 + i:121 + i]
                        link(dve.scalar_tensor_tensor(out=csum[:, i % 2, :], in0=csum[:, i % 2, :], scalar=0.5,
                                                      in1=cin[:, i % 3, 1:387], op0=ALU.mult, op1=ALU.subtract))
                        link(dve.scalar_tensor_tensor(out=cmix[:, i, 0:TP], in0=csum[:, i % 2, 0:TP], scalar=mu,
                                                 in1=cin[:, i % 3, 1:1 + TP], op0=ALU.mult, op1=ALU.add))
                        done(dve.scalar_tensor_tensor(out=cmix[:, i, TP:TOK], in0=csum[:, i % 2, TP + 2:TOK + 2], scalar=mu,
                                                 in1=cin[:, i % 3, 3 + TP:3 + TOK], op0=ALU.mult, op1=ALU.add
                                                 ), cmix_ready)
                    for key in qk_keys[0:5]:
                        ahead(key)

                    def take_values(n):
                        key = V_KEYS[n]
                        wait_group(dve, key)
                        freed(dve.tensor_copy(gu[:, n % 2, :], gbank(key)[:, 0:TOK]), key)

                    def take_turned(n):
                        dve.wait_ge(vt_done, n + 1)
                        key = ("vt", n)
                        dst = va[:, 0:NCH, :] if n == 0 else vb[:, 0:NCH, (n - 1) * 128:n * 128]
                        freed(dve.tensor_copy(dst, gbank(key)[:, 0:TOK].rearrange("p (c v) -> p c v", c=NCH)), key)

                    ahead(("av", 0))
                    dve.wait_ge(cmix_ready, C_BLOCKS)
                    take_values(0)
                    dve.wait_ge(lam_b, 1)
                    link(dve.tensor_copy(t2[:, 0:256], pb[3][:, 0:256]))
                    link(dve.tensor_tensor_reduce(t3[:, 0:64], t2[:, 0:64], t2[:, 64:128], 1.0, 0.0, ALU.mult, ALU.add, lam[:, 0:1]))
                    done(dve.tensor_tensor_reduce(t3[:, 64:128], t2[:, 128:192], t2[:, 192:256], 1.0, 0.0, ALU.mult, ALU.add,
                                             lam[:, 1:2]), lam_dot)
                    dve.wait_ge(kt_done, 1)
                    done(dve.tensor_copy(kc[:, 0:4, :].rearrange("p i t -> p (i t)"), pb[0][:, 0:512]), kc_ready)
                    dve.wait_ge(kt_done, 2)
                    done(dve.tensor_copy(kc[:, 4, :], pb[0][:, 0:128]), kc_ready)
                    dve.wait_ge(lam_exp, 1)
                    link(dve.tensor_tensor(lam[:, 4:5], lam[:, 2:3], lam[:, 3:4], ALU.subtract))
                    link(dve.tensor_tensor(lam[:, 5:6], lam[:, 4:5], small[:, 0:1], ALU.add))
                    link(dve.tensor_scalar(lam[:, 6:7], lam[:, 5:6], -1.0, None, ALU.mult))
                    link(dve.tensor_tensor(small[:, 4:5], par[:, 171:172], small[:, 1:2], ALU.mult))
                    take_turned(0)

                    def rope(i, bank):
                        dve.wait_ge(rot_done, i + 1)
                        ins = dve.tensor_tensor(rt[:, 0, :], cst[:, CO_SIN:CO_SIN + TS], bank[:, 0:TS], ALU.mult)
                        if i >= 5:
                            freed(ins, ("rot", i))
                        else:
                            link(ins)
                        link(dve.tensor_tensor(rt[:, 1, :], qk[:, i, TP:TOK], cst[:, CO_COS:CO_COS + TS], ALU.mult))
                        done(dve.tensor_tensor(qk[:, i, TP:TOK], rt[:, 0, :], rt[:, 1, :], ALU.add), rope_ready)

                    for i in range(6):
                        if i < 5:
                            ahead(B_QK[i])
                            dve.wait_ge(qstd_done, i + 1)
                            link(dve.reciprocal(t3[:, :], t2[:, :]))
                            gq = par[:, 172:173] if i < 4 else par[:, 173:174]
                            done(dve.scalar_tensor_tensor(out=qk[:, i, :], in0=qk[:, i, :], scalar=gq, in1=t3[:, :],
                                                     op0=ALU.mult, op1=ALU.mult), qn_ready)
                        if i >= 1:
                            rope(i - 1, pb[2 + (i - 1) % 2])
                    for key in B_QK[5:]:
                        ahead(key)
                    dve.wait_ge(swap_done, 1)
                    done(dve.tensor_copy(kswap[:, :], pb[0][:, :]), swap_ready)
                    dve.wait_ge(kout_t, 1)
                    done(dve.tensor_copy(kst[:, 0:4, :].rearrange("p i t -> p (i t)"), pb[1][:, 0:512]), kout_ready)
                    dve.wait_ge(kout_t, 2)
                    done(dve.tensor_copy(kst[:, 4, :], pb[1][:, 0:128]), kout_ready)

                    def maxima(un):
                        w = 128 if un["c"] == 0 else TOK
                        for n, _ in un["sets"]:
                            dve.wait_ge(scored, n + 1)
                            link(dve.reduce_max(st[:, n % 4, 0:1], pb[n % 2][:, 0:w], AX_X))
                            done(dve.tensor_scalar(st[:, n % 4, 1:2], st[:, n % 4, 0:1], -SCALE, None, ALU.mult), max_done)

                    def normalise(un):
                        w = 128 if un["c"] == 0 else TOK
                        for n, e in un["sets"]:
                            s, p = n % 4, pr[:, n % 4, 0:w]
                            dve.wait_ge(exp_done, n + 1)
                            link(dve.reciprocal(st[:, s, 3:4], st[:, s, 2:3]))
                            if un["tile"] < NB:
                                done(dve.tensor_scalar(p, p, st[:, s, 3:4], None, ALU.mult), probs_ready)
                            elif e == 0:
                                link(dve.tensor_scalar(p, p, st[:, s, 3:4], None, ALU.mult))
                            else:
                                link(dve.tensor_tensor(st[:, s, 3:4], st[:, s, 3:4], lam[:, 6:7], ALU.mult))
                                done(dve.scalar_tensor_tensor(out=p, in0=p, scalar=st[:, s, 3:4], in1=pr[:, (n - 1) % 4, 0:w],
                                                         op0=ALU.mult, op1=ALU.add), probs_ready)

                    def finish_a(un):
                        tile = un["tile"]
                        dve.wait_ge(branch_hi, tile + 1)
                        done(dve.scalar_tensor_tensor(out=br_lo[:, tile, :], in0=pb[3][:, 0:TOK], scalar=1.0,
                                                 in1=br_hi[:, tile, :].bitcast(F32), op0=ALU.mult, op1=ALU.subtract
                                                 ), branch_ready)

                    def sub_read(un):
                        dve.wait_ge(weighted_done, un["u"] + 1)
                        done(dve.tensor_copy(t2[:, :], pb[3][:, 0:TOK]), tile_read)

                    def sub_norm(un):
                        k = un["tile"] - NB + 1
                        dve.wait_ge(sub_std, k)
                        link(dve.reciprocal(t3[:, :], t3[:, :]))
                        done(dve.scalar_tensor_tensor(out=t2[:, :], in0=t2[:, :], scalar=small[:, 4:5], in1=t3[:, :],
                                                 op0=ALU.mult, op1=ALU.mult), sub_done)

                    def sub_low(un):
                        k = un["tile"] - NB
                        dve.wait_ge(branch_hi, NB + k + 1)
                        done(dve.tensor_tensor(br_lo[:, k, :], t2[:, :], br_hi[:, k, :].bitcast(F32), ALU.subtract), branch_ready)

                    def gate_up(br, m, gate, scratch):
                        uk = ("u", br, m)
                        wait_group(dve, uk)
                        if br == 0:
                            wait_freed(dve, ("g", 0, m))
                            freed(dve.scalar_tensor_tensor(out=merged[:, m, :], in0=merged[:, m, :], scalar=1.0,
                                                           in1=gbank(uk)[:, 0:TOK], op0=ALU.add, op1=ALU.mult), uk)
                        else:
                            wait_freed(dve, ("g", br, m))
                            freed(dve.scalar_tensor_tensor(out=scratch, in0=gate[:, m, :], scalar=1.0,
                                                           in1=gbank(uk)[:, 0:TOK], op0=ALU.add, op1=ALU.mult), uk)
                            done(dve.tensor_tensor(merged[:, m, :], merged[:, m, :], scratch, ALU.add), merged_done)

                    for u, un in enumerate(units):
                        maxima(un)
                        normalise(un)
                        sub = u >= 2 and units[u - 2]["last"] and units[u - 2]["tile"] >= NB
                        for key in fillers[u]:
                            if key[0] not in ("rot", "vt"):
                                ahead(key)
                        if sub:
                            sub_norm(units[u - 2])
                        for key in fillers[u]:
                            if key[0] == "bv":
                                take_values(key[1] + 1)
                            elif key[0] == "vt":
                                take_turned(key[1])
                            elif key[0] == "rot":
                                rope(key[1], gbank(key))
                            elif key[0] == "u":
                                for e in range(2):
                                    gate_up(0, 2 * key[2] + e, None, None)
                        if sub:
                            sub_low(units[u - 2])
                        if u >= 1 and units[u - 1]["last"]:
                            (finish_a if units[u - 1]["tile"] < NB else sub_read)(units[u - 1])
                    sub_read(units[-1])
                    sub_norm(units[-1])
                    sub_low(units[-1])
                    for mp in range(KD // 2):
                        ahead(("u", 1, mp))
                        for e in range(2):
                            gate_up(1, 2 * mp + e, gate1, gu[:, e, :])

                    dve.wait_ge(kv_out, 64)
                    for c in range(NCH):
                        dve.wait_ge(vtok_t, c + 1)
                        done(dve.tensor_copy(vtok[:, c, :], pb[c][:, :]), vtok_ready)

                    def chunked(t):
                        return t[:, :].rearrange("p (c t) -> p c t", c=NCH)

                    def prepare_raw(j):
                        done(dve.tensor_scalar(kk[:, :], cmix[:, 4 + j, :], par[:, 151 + j:152 + j], None, ALU.mult), kk_raw)

                    def prepare_norm(j):
                        dve.wait_ge(kk_std, j + 1)
                        link(dve.reciprocal(bt[:, :], bt[:, :]))
                        link(dve.tensor_tensor(kk[:, :], kk[:, :], bt[:, :], ALU.mult))

                    def prepare_sums(g):
                        d = g % 2
                        dve.wait_ge(sg_done, g + 1)
                        for c in range(NCH):
                            t = slice(c * 128, (c + 1) * 128)
                            ins = dve.tensor_tensor_scan(cs[:, t], ones, sg[:, t], 0.0, ALU.mult, ALU.add)
                        link(ins)
                        link(dve.tensor_scalar(half[:, :], chunked(cs)[:, :, 127], 0.5, None, ALU.mult))
                        for c in range(NCH):
                            t = slice(c * 128, (c + 1) * 128)
                            if d == 0:
                                ins = dve.tensor_scalar(zi[:, t], cs[:, t], half[:, c:c + 1], None, ALU.subtract)
                            else:
                                ins = dve.tensor_scalar(zx[:, t], cs[:, t], -1.0, half[:, c:c + 1], ALU.mult, ALU.add)
                        link(ins)
                        if d == 0:
                            done(dve.tensor_tensor(zx[:, :], zi[:, :], sg[:, :], ALU.subtract), z_ready)
                        else:
                            done(dve.tensor_tensor(zi[:, :], zx[:, :], sg[:, :], ALU.add), z_ready)

                    def prepare_keys(g):
                        j, d = g // 2, g % 2
                        link(dve.tensor_scalar(cs[:, :], aa[:, :], par[:, 155 + j:156 + j], small[:, 8 + j:9 + j], ALU.mult, ALU.add))
                        link(dve.tensor_tensor(kt[:, :], cs[:, :], cmix[:, 4 + j, :], ALU.mult))
                        if d == 0:
                            link(dve.tensor_copy(ksum[:, j % 2, :], kt[:, :]))
                        else:
                            link(dve.tensor_tensor(ksum[:, j % 2, :], ksum[:, j % 2, :], kt[:, :], ALU.add))
                        link(dve.tensor_tensor(aa[:, :], aa[:, :], kk[:, :], ALU.mult))

                    def prepare_decayed(g):
                        j = g // 2
                        dve.wait_ge(exps_done, g + 1)
                        link(dve.scalar_tensor_tensor(out=ar[:, g % 2, :, 0, :], in0=chunked(kk), scalar=-1.0, in1=chunked(zx),
                                                 op0=ALU.mult, op1=ALU.mult))
                        link(dve.tensor_tensor(ar[:, g % 2, :, 1, :], cmix[:, j, :].rearrange("p (c t) -> p c t", c=NCH),
                                               chunked(sg), ALU.mult))
                        link(dve.tensor_tensor(bt[:, :], aa[:, :], zi[:, :], ALU.mult))
                        done(dve.tensor_tensor(kt[:, :], kt[:, :], zi[:, :], ALU.mult), ab_ready)

                    def prepare_gram(g, f):
                        d, n = g % 2, 6 * g + f
                        dve.wait_ge(lt_ready, n + 1)
                        u = 3 * (f % 2) + f // 2
                        src = acc[n % 2][:, :].rearrange("p (i a t) -> p i a t", i=2, a=2)
                        link(dve.tensor_tensor(lak[:, g % 2, u, :], src[:, 1, 0, :],
                                          cst[:, CO_STR + 128 * d:CO_STR + 128 * d + 128], ALU.mult))
                        done(dve.tensor_tensor(rbk[:, g % 2, u, :, :], src[:, :, 1, :],
                                          over(cst[:, CO_INC + 128 * d:CO_INC + 128 * d + 128], 2), ALU.mult
                                          ), gram_read)

                    def first_level(g):
                        o = CO_LEV + (g % 2) * len(LEVELS) * 128
                        dve.wait_ge(lt_ready, 6 * g + 6)
                        link(dve.tensor_tensor(xt[:, g % 2, :, :], lt[g % 2][:, :, :], over(cst[:, o:o + 128], 6), ALU.mult))

                    def first_level_done(g):
                        done(dve.tensor_tensor(xt[:, g % 2, :, :], xt[:, g % 2, :, :], over(ident, 6), ALU.add), xt0_ready)

                    def level_add(g, n):
                        for h in range(2):
                            dve.wait_ge(u_done, 2 * (NL * g + n - 1) + h + 1)
                            half_x = xi[:, 3 * h:3 * h + 3, :].rearrange("p u s -> p (u s)")
                            done(dve.tensor_tensor(half_x, half_x, pb[h][:, 0:TOK], ALU.add), xi_ready)

                    def scan_start(g):
                        dve.wait_ge(state_t, g + 1)
                        c1 = scan_order(g)[1]
                        done(dve.tensor_scalar(sp[:, :], acc[1][:, 0:128], eh[:, g % 2, c1:c1 + 1], None, ALU.mult), sp_ready)

                    def scan_solve(g, i):
                        dve.wait_ge(sa_done, 3 * g + i + 1)
                        done(dve.tensor_copy(sas[:, :], acc[0][:, 128:256]), sa_ready)

                    def scan_out(g, i):
                        c, n = scan_order(g)[i], 3 * g + i
                        t = slice(c * 128, (c + 1) * 128)
                        dve.wait_ge(o_done, n + 1)
                        if g % 2 == 0:
                            done(dve.tensor_copy(osum[:, t], acc[2][:, 0:128]), o_read)
                        else:
                            done(dve.tensor_tensor(osum[:, t], osum[:, t], acc[2][:, 0:128], ALU.add), o_read)
                        if i < 2:
                            dve.wait_ge(sn_done, 2 * g + i + 1)
                            for hh in range(2):
                                hs = slice(64 * hh, 64 * hh + 64)
                                if i == 0:
                                    ins = dve.tensor_scalar(spo[hs, hs], acc[3][hs, hs], eh[hs, g % 2, 0:1], None, ALU.mult)
                                else:
                                    ins = dve.tensor_tensor(sp[hs, hs], sp[hs, hs], acc[3][hs, hs], ALU.add)
                            if i == 0:
                                done(ins, sn_read)
                            else:
                                link(ins)
                                c1, c2 = scan_order(g)[1:3]
                                done(dve.tensor_scalar(sp[:, :], sp[:, :], eh[:, g % 2, c1:c1 + 1], eh[:, g % 2, c2:c2 + 1],
                                                  ALU.mult, ALU.mult), sp_ready)

                    def tile_bonus(j):
                        done(dve.scalar_tensor_tensor(out=guc[:, 0, :], in0=cmix[:, j, :], scalar=par[:, 159 + j:160 + j],
                                                 in1=ksum[:, j % 2, :], op0=ALU.mult, op1=ALU.mult), bonus_in)

                    def tile_centre(j):
                        dve.wait_ge(gn_mean, j + 1)
                        done(dve.scalar_tensor_tensor(out=osum[:, :], in0=acc[2][:, 0:TOK], scalar=-1.0 / HD, in1=osum[:, :],
                                                 op0=ALU.mult, op1=ALU.add), gn_centred)
                        dve.wait_ge(bonus_sum, j + 1)
                        done(dve.tensor_tensor(guc[:, 0, :], cmix[:, 8 + j, :], acc[3][:, 0:TOK], ALU.mult), bonus_read)

                    def tile_norm(j):
                        dve.wait_ge(gn_std, j + 1)
                        link(dve.reciprocal(guc[:, 1, :], guc[:, 1, :]))
                        link(dve.tensor_tensor(osum[:, :], osum[:, :], guc[:, 1, :], ALU.mult))
                        link(dve.tensor_scalar(osum[:, :], osum[:, :], par[:, 163 + j:164 + j], par[:, 167 + j:168 + j],
                                               ALU.mult, ALU.add))
                        link(dve.tensor_tensor(osum[:, :], osum[:, :], guc[:, 0, :], ALU.add))
                        dve.wait_ge(out_gate, j + 1)
                        done(dve.tensor_tensor(osum[:, :], osum[:, :], acc[3][:, 0:TOK], ALU.mult), out_done)

                    def tile_low(j):
                        dve.wait_ge(brc_hi_s, j + 1)
                        done(dve.tensor_tensor(brc_lo[:, j, :], osum[:, :], brc_hi[:, j, :].bitcast(F32), ALU.subtract
                                          ), brc_ready)

                    prepare_raw(0)
                    prepare_norm(0)
                    prepare_sums(0)
                    prepare_keys(0)
                    prepare_decayed(0)
                    for f in range(6):
                        prepare_gram(0, f)
                    first_level(0)
                    first_level_done(0)
                    for g in range(2 * NB + 1):
                        inv, scan, nxt = g < 2 * NB, g >= 1, g + 1 < 2 * NB
                        tail = scan and g % 2 == 0
                        for n in range(1, NL + 1):
                            if nxt and n == 1 and g % 2 == 1:
                                prepare_raw((g + 1) // 2)
                            if scan and n == 1:
                                scan_start(g - 1)
                            if tail and n == 4:
                                tile_centre(g // 2 - 1)
                            if nxt and n == 5:
                                prepare_gram(g + 1, 0)
                                prepare_gram(g + 1, 1)
                            if nxt and n == 6:
                                first_level(g + 1)
                            if inv:
                                level_add(g, n)
                            if nxt and n == 6:
                                first_level_done(g + 1)
                            if g >= 3 and g % 2 == 1 and n == 1:
                                tile_low(g // 2 - 1)
                            if scan and n <= 3:
                                scan_solve(g - 1, n - 1)
                            if nxt and n == 3:
                                prepare_sums(g + 1)
                            if scan and n <= 3:
                                scan_out(g - 1, n - 1)
                            if tail and n == 3:
                                tile_bonus(g // 2 - 1)
                            if nxt and n == 2 and g % 2 == 1:
                                prepare_norm((g + 1) // 2)
                            if nxt and n == 3:
                                prepare_keys(g + 1)
                            if nxt and n == 4:
                                prepare_decayed(g + 1)
                            if nxt and n == 5:
                                for f in range(2, 6):
                                    prepare_gram(g + 1, f)
                            if tail and n == 6:
                                tile_norm(g // 2 - 1)
                    tile_low(NB - 1)
                    dve.wait_ge(st_out, 16 * 4 * NB)
                    for mp in range(KD // 2):
                        ahead(("u", 2, mp))
                        for e in range(2):
                            gate_up(2, 2 * mp + e, gate2, guc[:, e, :])
                    for m in range(KD):
                        dve.wait_ge(xhi_ready, 2 * KD + m + 1)
                        done(dve.scalar_tensor_tensor(out=xm_lo[:, m, :], in0=merged[:, m, :], scalar=0.5,
                                                      in1=xm_hi[:, m, :].bitcast(F32), op0=ALU.mult, op1=ALU.subtract), xm_ready)
                    for m in range(KD):
                        ahead(("w", m))
                        residual(1, ("w", m), m)
                    layer_norm(1)
                    modulate(2, 3)
                    ffn(1)
            nc.multi_engine_barrier([e.engine for e in (nc.sync, nc.scalar, nc.vector, nc.tensor, nc.gpsimd)],
                                    sems_to_clear=range(sems[0].num, sems[-1].num + 1))

        with nc.Block() as block:
            @block.tensor
            def _(pe):
                for c in range(NCH):
                    for hf_ in range(2):
                        n = 2 * c + hf_
                        if n >= 4:
                            pe.wait_ge(fin_cp, n - 3)
                        for k in range(4):
                            mm = pe.transpose(pb[n % 4][:, k * 128:(k + 1) * 128], x[:, 4 * hf_ + k, c * 128:(c + 1) * 128], ident)
                        mm.then_inc(fin_t, 1)

            @block.vector
            def _(dve):
                for n in range(2 * NCH):
                    dve.wait_ge(fin_t, n + 1)
                    dve.tensor_copy(xrows[:, n // 2, (n % 2) * 512:(n % 2) * 512 + 512], pb[n % 4][:, :]).then_inc(fin_cp, 1)

            @block.sync
            def _(sy):
                sy.wait_ge(fin_cp, 2)
                sy.dma_start(O["y_prompt"][0], xrows[:, 0, :]).then_inc(y_out, 16)
                sy.wait_ge(fin_cp, 2 * NCH)
                sy.dma_start(O["y_sample"][0].rearrange("(c p) d -> p c d", p=128), xrows[:, 1:3, :]).then_inc(y_out, 16)
                sy.wait_ge(y_out, 32)


_OUTS = {"y_prompt": (1, TP, D), "y_sample": (1, TS, D), "new_attn_k": (1, DEPTH, 2, TP, HD), "new_attn_v": (1, DEPTH, 2, TP, HD),
         "new_diff_k": (1, DEPTH, 4, TP, 128), "new_diff_v": (1, DEPTH, 4, TP, 128),
         "new_state": (1, DEPTH, 2, 8, HD, HD)}
_LAYER_VIEWS = {"cache_attn_k": "cache_attn_k_l", "cache_attn_v": "cache_attn_v_l", "cache_diff_k": "cache_diff_k_l",
                "cache_diff_v": "cache_diff_v_l", "state_rwkv": "state_rwkv_l"}


def kernel(**inputs):
    import numpy as _np
    import concourse.bacc as _bacc
    from concourse import mybir as _mybir
    from concourse.bass_utils import run_bass_kernel_spmd as _run

    nc = _bacc.Bacc("TRN2", target_bir_lowering=False, num_devices=1)
    arrays, I, O = {}, {}, {}
    for name, a in dict(inputs, const=shape_constants()).items():
        a = _np.ascontiguousarray(a)
        arrays[f"in_{name}"] = a
        I[name] = nc.dram_tensor(f"in_{name}", a.shape, _mybir.dt.from_np(a.dtype), kind="ExternalInput").ap()
        if name in _LAYER_VIEWS:
            I[_LAYER_VIEWS[name]] = I[name][0]
    for name, shape in _OUTS.items():
        O[name] = nc.dram_tensor(f"out_{name}", shape, _mybir.dt.float32, kind="ExternalOutput").ap()
        O[name + "_l"] = O[name][0]
    build(nc, I, O)
    r = _run(nc, [arrays], core_ids=[0])
    return tuple(r.results[0][f"out_{name}"] for name in _OUTS)
```
